# Optimizing a Trainium2 kernel written in Bass

```python
import jax, jax.numpy as jnp
from jax import lax
import numpy as np

D_MODEL = 2048
BATCH = 1
SEQ = 512
DEPTH = 1
DEC_BATCH = 8
DEC_SEQ = 1
PAST_LEN = 4096
PAGE_SIZE = 128

MIX_WIDTH = D_MODEL
W_LRU = MIX_WIDTH // 2
LRU_HEADS = 8
LRU_HD = W_LRU // LRU_HEADS
CONV_W = 4
LRU_C = 8.0
W_POOL = MIX_WIDTH - W_LRU
POOL_WINDOWS = (2, 4, 8, 16)
POOL_GROUPS = len(POOL_WINDOWS)
POOL_GD = W_POOL // POOL_GROUPS
POOL_BUF = max(POOL_WINDOWS) - 1
D_FF = 4 * D_MODEL
EPS = 1e-6

kernel_name = "hymba_rglru_pool_decode_step"

def rmsnorm(x, g):
    xf = x.astype(jnp.float32)
    y = xf * lax.rsqrt(jnp.mean(xf * xf, axis=-1, keepdims=True) + EPS)
    return (y * g.astype(jnp.float32)).astype(x.dtype)

def causal_conv(u, buf, w, b):
    T = u.shape[1]
    ext = jnp.concatenate([buf.astype(jnp.float32), u.astype(jnp.float32)], axis=1)
    out = b.astype(jnp.float32)
    for k in range(CONV_W):
        out = out + ext[:, k:k + T] * w[k].astype(jnp.float32)
    return out, ext[:, -(CONV_W - 1):].astype(u.dtype)

def rg_lru(x, h0, pos, w_a, b_a, w_x, b_x, lam):
    B, T, _ = x.shape
    xh = x.reshape(B, T, LRU_HEADS, LRU_HD)
    r = jax.nn.sigmoid(jnp.einsum('bthi,hij->bthj', xh, w_a.astype(jnp.float32)).reshape(B, T, W_LRU) + b_a.astype(jnp.float32))
    i = jax.nn.sigmoid(jnp.einsum('bthi,hij->bthj', xh, w_x.astype(jnp.float32)).reshape(B, T, W_LRU) + b_x.astype(jnp.float32))
    log_a = -LRU_C * r * jax.nn.softplus(-lam.astype(jnp.float32))
    a = jnp.exp(log_a)
    mult = jnp.sqrt(1.0 - jnp.exp(2.0 * log_a))
    mult = jnp.where((pos == 0)[None, :, None], 1.0, mult)
    bx = x * i * mult

    def combine(l, rr):
        a1, b1 = l
        a2, b2 = rr
        return a1 * a2, a2 * b1 + b2

    a_cum, b_cum = lax.associative_scan(combine, (a, bx), axis=1)
    h = a_cum * h0.astype(jnp.float32)[:, None, :] + b_cum
    return h, h[:, -1]

def pool_mix(u, buf, pos, w_pool, scale):
    B, T, _ = u.shape
    ext = jnp.concatenate([buf.astype(jnp.float32), u.astype(jnp.float32)], axis=1)
    cs0 = jnp.concatenate([jnp.zeros((B, 1, W_POOL), jnp.float32), jnp.cumsum(ext, axis=1)], axis=1)
    start = POOL_BUF + 1
    cur = ext[:, POOL_BUF:]
    outs = []
    for g, w in enumerate(POOL_WINDOWS):
        sl = slice(g * POOL_GD, (g + 1) * POOL_GD)
        wsum = cs0[:, start:start + T, sl] - cs0[:, start - w:start - w + T, sl]
        count = jnp.minimum(pos + 1, w).astype(jnp.float32)[None, :, None]
        outs.append(wsum / count - cur[:, :, sl])
    pooled = jnp.stack(outs, axis=2)
    y = jnp.einsum('btgi,gij->btgj', pooled, w_pool.astype(jnp.float32)).reshape(B, T, W_POOL)
    y = y * scale.astype(jnp.float32)
    return y, ext[:, -POOL_BUF:].astype(u.dtype)

def layer(x, lru_h0, conv_buf, pool_buf, pos, norm_mix_g, w_in, conv_w, conv_b, w_rg_a, b_rg_a,
          w_rg_x, b_rg_x, lru_lambda, w_pool, pool_scale, w_out, norm_mlp_g, w_up, w_down):
    h = rmsnorm(x, norm_mix_g)
    proj = jnp.einsum('btd,de->bte', h, w_in)
    u_x = proj[..., :W_LRU]
    u_gate = proj[..., W_LRU:2 * W_LRU]
    u_pool = proj[..., 2 * W_LRU:]
    xc, new_conv = causal_conv(u_x, conv_buf, conv_w, conv_b)
    hs, h_last = rg_lru(xc, lru_h0, pos, w_rg_a, b_rg_a, w_rg_x, b_rg_x, lru_lambda)
    y_lru = hs * jax.nn.gelu(u_gate.astype(jnp.float32), approximate=True)
    y_pool, new_pool = pool_mix(u_pool, pool_buf, pos, w_pool, pool_scale)
    y_mix = jnp.concatenate([y_lru, y_pool], axis=-1).astype(x.dtype)
    x = x + jnp.einsum('bte,ed->btd', y_mix, w_out)
    h2 = rmsnorm(x, norm_mlp_g)
    f = jax.nn.relu(jnp.einsum('btd,df->btf', h2, w_up))
    x = x + jnp.einsum('btf,fd->btd', f * f, w_down)
    return x, h_last.astype(x.dtype), new_conv, new_pool

def setup_inputs(seed: int = 0) -> dict:
    key = jax.random.key(seed)
    ks = jax.random.split(key, 24)
    f32 = jnp.float32
    nrm = lambda k, s, sc: jax.random.normal(k, s, f32) * sc
    a0 = jax.random.uniform(ks[10], (DEPTH, W_LRU), f32, 0.9, 0.999)
    base = a0 ** (1.0 / LRU_C)
    lru_lambda = jnp.log(base) - jnp.log1p(-base)
    return {
        "x_prompt": nrm(ks[0], (BATCH, SEQ, D_MODEL), 1.0),
        "x_sample": nrm(ks[1], (DEC_BATCH, DEC_SEQ, D_MODEL), 1.0),
        "state_lru_h": nrm(ks[2], (DEPTH, DEC_BATCH, W_LRU), 0.5),
        "state_conv": nrm(ks[3], (DEPTH, DEC_BATCH, CONV_W - 1, W_LRU), 1.0),
        "state_pool": nrm(ks[4], (DEPTH, DEC_BATCH, POOL_BUF, W_POOL), 1.0),
        "norm_mix_g": 1.0 + nrm(ks[5], (DEPTH, D_MODEL), 0.02),
        "w_in": nrm(ks[6], (DEPTH, D_MODEL, 2 * W_LRU + W_POOL), D_MODEL ** -0.5),
        "conv_w": nrm(ks[7], (DEPTH, CONV_W, W_LRU), CONV_W ** -0.5),
        "conv_b": nrm(ks[8], (DEPTH, W_LRU), 0.01),
        "w_rg_a": nrm(ks[9], (DEPTH, LRU_HEADS, LRU_HD, LRU_HD), LRU_HD ** -0.5),
        "b_rg_a": nrm(ks[11], (DEPTH, W_LRU), 0.01),
        "w_rg_x": nrm(ks[12], (DEPTH, LRU_HEADS, LRU_HD, LRU_HD), LRU_HD ** -0.5),
        "b_rg_x": nrm(ks[13], (DEPTH, W_LRU), 0.01),
        "lru_lambda": lru_lambda,
        "w_pool": nrm(ks[14], (DEPTH, POOL_GROUPS, POOL_GD, POOL_GD), POOL_GD ** -0.5),
        "pool_scale": 0.5 + nrm(ks[15], (DEPTH, W_POOL), 0.05),
        "w_out": nrm(ks[16], (DEPTH, MIX_WIDTH, D_MODEL), MIX_WIDTH ** -0.5),
        "norm_mlp_g": 1.0 + nrm(ks[17], (DEPTH, D_MODEL), 0.02),
        "w_up": nrm(ks[18], (DEPTH, D_MODEL, D_FF), D_MODEL ** -0.5),
        "w_down": nrm(ks[19], (DEPTH, D_FF, D_MODEL), D_FF ** -0.5),
        "norm_final_g": 1.0 + nrm(ks[20], (D_MODEL,), 0.02),
    }

def reference(x_prompt, x_sample, state_lru_h, state_conv, state_pool, norm_mix_g, w_in, conv_w, conv_b,
              w_rg_a, b_rg_a, w_rg_x, b_rg_x, lru_lambda, w_pool, pool_scale, w_out, norm_mlp_g,
              w_up, w_down, norm_final_g):
    Bp, Tp, _ = x_prompt.shape
    Bs, Ts, _ = x_sample.shape
    pos_p = jnp.arange(Tp, dtype=jnp.int32)
    pos_s = PAST_LEN + jnp.arange(Ts, dtype=jnp.int32)
    xp, xs = x_prompt, x_sample
    hp_l, cp_l, pp_l, hs_l, cs_l, ps_l = [], [], [], [], [], []
    for l in range(DEPTH):
        wts = (norm_mix_g[l], w_in[l], conv_w[l], conv_b[l], w_rg_a[l], b_rg_a[l], w_rg_x[l], b_rg_x[l],
               lru_lambda[l], w_pool[l], pool_scale[l], w_out[l], norm_mlp_g[l], w_up[l], w_down[l])
        h0 = jnp.zeros((Bp, W_LRU), jnp.float32)
        cb0 = jnp.zeros((Bp, CONV_W - 1, W_LRU), xp.dtype)
        pb0 = jnp.zeros((Bp, POOL_BUF, W_POOL), xp.dtype)
        xp, hp, cp, pp = layer(xp, h0, cb0, pb0, pos_p, *wts)
        xs, hs, cs, ps = layer(xs, state_lru_h[l], state_conv[l], state_pool[l], pos_s, *wts)
        hp_l.append(hp); cp_l.append(cp); pp_l.append(pp)
        hs_l.append(hs); cs_l.append(cs); ps_l.append(ps)
    y_prompt = rmsnorm(xp, norm_final_g)
    y_sample = rmsnorm(xs, norm_final_g)
    return (y_prompt, y_sample, jnp.stack(hp_l), jnp.stack(cp_l), jnp.stack(pp_l),
            jnp.stack(hs_l), jnp.stack(cs_l), jnp.stack(ps_l))


_drawn_inputs = setup_inputs


def setup_inputs(seed=0):
    import zlib

    import numpy as np

    out = dict(_drawn_inputs(seed))
    spreads = {}
    factors = {'b_rg_a': 23.486, 'b_rg_x': 8.0, 'norm_mlp_g': 3.25, 'norm_final_g': 8.248}
    for name, (base, spread) in spreads.items():
        noise = np.random.default_rng([zlib.crc32(name.encode()), seed]).standard_normal(out[name].shape)
        drawn = base * np.exp(spread * noise) if base else spread * noise
        out[name] = __import__('jax').numpy.asarray(drawn.astype(out[name].dtype))
    for name, factor in factors.items():
        out[name] = (out[name] * factor).astype(out[name].dtype)
    return out
```

```python
from contextlib import ExitStack

import concourse.bass as bass
from concourse import mybir

F32 = mybir.dt.float32
F32R = mybir.dt.float32r
ALU = mybir.AluOpType
ACT = mybir.ActivationFunctionType
AX_X = mybir.AxisListType.X

P = 128
D = 2048
KC = D // P
PROMPT = 512
SAMPLES = 8
TOK = PROMPT + SAMPLES
HALF = TOK // 2
W_LRU = 1024
HEADS = W_LRU // P
CONV_W = 4
WINDOWS = (2, 4, 8, 16)
POOL_BUF = 15
GROUPS = 4
EPS = 1e-6
UNIT = 2 * 256
RING = 4
PAIR_UNITS = 8
IN_PAIRS, OUT_PAIRS, MLP_PAIRS = 12, 8, 8
SQRT_2_OVER_PI = 0.7978845608028654
GELU_CUBIC = 0.044715

EXT = 3 + TOK + CONV_W * SAMPLES + 1
EXT_S = 3 + TOK
CONV = EXT_S + CONV_W * (SAMPLES - 1) + 1
PEXT = POOL_BUF + TOK + (POOL_BUF + 1) * SAMPLES
PEXT_S = POOL_BUF + TOK

ROWS_OF = {}
_at = 0
for _name, _n in (("g_mix", KC), ("g_mlp", KC), ("g_final", KC), ("conv_w", CONV_W * HEADS), ("conv_b", HEADS),
                  ("b_a", HEADS), ("b_x", HEADS), ("lam", HEADS), ("pool_scale", HEADS)):
    ROWS_OF[_name] = _at
    _at += _n
VECTORS = _at

ST_LRU, ST_CONV = 0, SAMPLES * HEADS
ST_POOL = ST_CONV + SAMPLES * 3 * HEADS
ST_COLS = ST_POOL + SAMPLES * POOL_BUF * HEADS


class Order:

    def __init__(self, eng, sem):
        self.eng, self.sem, self.count, self.shift = eng, sem, 0, 0

    def mark(self, ins):
        ins.then_inc(self.sem, 1)
        self.count += 1

    def settle(self):
        self.eng.wait_ge(self.sem, self.shift + self.count)

    def enter(self, turn, per_turn):
        self.saved, self.base, self.per_turn = self.shift, self.count, per_turn
        self.shift = self.shift + turn * per_turn

    def leave(self, turns):
        assert self.count - self.base == self.per_turn, (self.count - self.base, self.per_turn)
        self.shift, self.count = self.saved, self.base + turns * self.per_turn


def build(nc, x_prompt, x_sample, state_lru_h, state_conv, state_pool, norm_mix_g, w_in, conv_w, conv_b,
          w_rg_a, b_rg_a, w_rg_x, b_rg_x, lru_lambda, w_pool, pool_scale, w_out, norm_mlp_g, w_up, w_down,
          norm_final_g, y_prompt, y_sample, lru_prompt, conv_prompt, pool_prompt, lru_sample, conv_sample,
          pool_sample):
    with ExitStack() as ctx:
        def sb(name, shape, dt=F32):
            return ctx.enter_context(nc.sbuf_tensor(name, shape, dt))

        def sem(name):
            return ctx.enter_context(nc.semaphore(name))

        h_high = sb("h_high", [P, KC, TOK], F32R)
        h_low = sb("h_low", [P, KC, TOK], F32R)
        y_high = sb("y_high", [P, KC, TOK], F32R)
        y_low = sb("y_low", [P, KC, TOK], F32R)
        resid = sb("resid", [P, KC, TOK])
        raw = sb("raw", [P, RING, UNIT])
        w_high = sb("w_high", [P, RING, 2, 256], F32R)
        w_low = sb("w_low", [P, RING, 2, 256], F32R)
        aux_raw = sb("aux_raw", [P, UNIT])
        aux_high = sb("aux_high", [P, UNIT], F32R)
        aux_low = sb("aux_low", [P, UNIT], F32R)
        rstd = sb("rstd", [P, TOK])
        scratch = sb("scratch", [P, 4, TOK])
        ident = sb("ident", [P, P])
        ones = sb("ones", [P, P])
        vec = sb("vec", [P, P])
        half_bias = sb("half_bias", [P, 2 * HEADS])
        lru_c = sb("lru_c", [P, 2, HEADS])
        tiny = sb("tiny", [P, 4, HEADS])
        xs_t = sb("xs_t", [P, P])
        xs_rows = sb("xs_rows", [P, P])
        inv_count = sb("inv_count", [P, POOL_BUF])
        sumsq = sb("sumsq", [P, 5])
        sel = sb("sel", [P, SAMPLES])
        lru_last = sb("lru_last", [P, 1 + SAMPLES, HEADS])
        conv_last = sb("conv_last", [P, 3 + SAMPLES, HEADS])
        pool_last = sb("pool_last", [P, POOL_BUF + SAMPLES, HEADS])
        r_final = sb("r_final", [P, 4, 5])
        ps = ctx.enter_context(nc.psum_tensor("ps", [P, 8, 512], F32))

        flat = resid[:].rearrange("p k t -> p (k t)")
        x_rows = flat[:, 0:4 * D].rearrange("p (t d) -> p t d", t=4)
        state_rows = flat[:, 0:11 * P].rearrange("p (n f) -> p n f", n=11)
        at = [0]

        def work(cols):
            at[0] += 2 * cols
            return flat[:, at[0] - 2 * cols:at[0]].rearrange("p (h t) -> p h t", h=2)

        conv_in = work(EXT)
        q = flat[:, 0:2 * TOK].rearrange("p (h t) -> p h t", h=2)
        conv_sum = work(CONV)
        gate = flat[:, 2 * EXT:2 * EXT + 2 * TOK].rearrange("p (h t) -> p h t", h=2)
        xc, tanh_x, tanh_a, decay = work(TOK), work(TOK), work(TOK), work(TOK)
        states = flat[:, at[0]:at[0] + ST_COLS]
        assert at[0] + ST_COLS <= KC * TOK
        at[0] = 0
        pool_in, sum_a, sum_b = work(PEXT), work(PEXT), work(PEXT)
        pooled, head_fix = work(TOK), work(POOL_BUF)
        x_t_dram = nc.dram_tensor("x_t_spill", (KC, P, PROMPT), F32).ap()

        vectors_in, xs_in, states_in = sem("vectors_in"), sem("xs_in"), sem("states_in")
        x_in = [sem(f"x_in{t}") for t in range(4)]
        raw_in = [sem(f"raw_in{s}") for s in range(RING)]
        loads = sem("loads")
        aux_in, aux_hi, aux_lo = sem("aux_in"), sem("aux_hi"), sem("aux_lo")
        hi_ready, lo_ready, unit_used = sem("hi_ready"), sem("lo_ready"), sem("unit_used")
        ident_ready = sem("ident_ready")
        small_t, small_copied = sem("small_t"), sem("small_copied")
        x_t, x_hi, x_lo, x_staged = sem("x_t"), sem("x_hi"), sem("x_lo"), sem("x_staged")
        xs_scaled, xs_hi, xs_lo = sem("xs_scaled"), sem("xs_hi"), sem("xs_lo")
        spilled = [sem(f"spilled{s}") for s in range(4)]
        sumsq_ready, diag_ready, total_ready = sem("sumsq_ready"), sem("diag_ready"), sem("total_ready")
        mean_ready, root_ready = sem("mean_ready"), sem("root_ready")
        states_t, states_copied = sem("states_t"), sem("states_copied")
        lam_ready, lam_tanh = sem("lam_ready"), sem("lam_tanh")
        vec_order, act_order = sem("vector_order"), sem("scalar_order")
        ext_ready, tap0_ready, xc_ready = sem("ext_ready"), sem("tap0_ready"), sem("xc_ready")
        xc_hi, xc_lo, gates_mm = sem("xc_hi"), sem("xc_lo"), sem("gates_mm")
        gates_tanh, decay_exp, decay_tanh = sem("gates_tanh"), sem("decay_exp"), sem("decay_tanh")
        xi_ready, tanh_used, root_t = sem("xi_ready"), sem("tanh_used"), sem("root_t")
        gate_evac, gate_sq, gate_arg, gate_th = sem("gate_evac"), sem("gate_sq"), sem("gate_arg"), sem("gate_th")
        lru_y, y_hi, y_lo = sem("lru_y"), sem("y_hi"), sem("y_lo")
        pooled_ready, pooled_hi, pooled_lo, pool_mm = (sem("pooled_ready"), sem("pooled_hi"), sem("pooled_lo"),
                                                       sem("pool_mm"))
        last_ready, last_t, last_copied = sem("last_ready"), sem("last_t"), sem("last_copied")
        x_back = sem("x_back")
        pair_evac = sem("pair_evac")
        h2_hi, h2_lo, out_sq = sem("h2_hi"), sem("h2_lo"), sem("out_sq")
        sq_summed = sem("sq_summed")
        f_relu, f_sq, f_hi, f_lo = sem("f_relu"), sem("f_sq"), sem("f_hi"), sem("f_lo")
        final_sq, final_scaled, final_total = sem("final_sq"), sem("final_scaled"), sem("final_total")
        final_rstd, y_t, y_even, y_odd = sem("final_rstd"), sem("y_t"), sem("y_even"), sem("y_odd")
        y_stored = [sem(f"y_stored{s}") for s in range(RING)]
        states_stored = sem("states_stored")

        def bank(buf, tile):
            return ps[:, 4 * buf + 2 * tile:4 * buf + 2 * tile + 2, 0:HALF]

        def halves(v):
            return v.rearrange("p (a t) -> p a t", a=2)

        def column(name, c, step=None):
            return vec[:, bass.ds(ROWS_OF[name] + c, 1)]

        w_in_v = w_in[0].rearrange("(k p) e -> p k e", p=P)
        w_out_v = w_out[0].rearrange("(k p) e -> p k e", p=P)
        w_up_v = w_up[0].rearrange("(k p) e -> p k e", p=P)
        w_down_v = w_down[0].rearrange("(k p) e -> p k e", p=P)

        def pool_group(n):
            return len(WINDOWS) - 1 - n

        def y_row(slot):
            return slot if slot < HEADS else HEADS + 2 * pool_group((slot - HEADS) // 2) + slot % 2

        block = ctx.enter_context(nc.Block())

        @block.sync
        def _(sp):
            for name, src in (("g_mix", norm_mix_g[0]), ("g_mlp", norm_mlp_g[0]), ("g_final", norm_final_g),
                              ("conv_b", conv_b[0]), ("b_a", b_rg_a[0]), ("b_x", b_rg_x[0]),
                              ("lam", lru_lambda[0]), ("pool_scale", pool_scale[0])):
                rows = src.rearrange("(c f) -> c f", f=P)
                a = ROWS_OF[name]
                sp.dma_start(aux_raw[a:a + rows.shape[0], 0:P], rows).then_inc(vectors_in, 16)
            a = ROWS_OF["conv_w"]
            sp.dma_start(aux_raw[a:a + CONV_W * HEADS, 0:P],
                         conv_w[0].rearrange("k (c f) -> (k c) f", f=P)).then_inc(vectors_in, 16)
            sp.dma_start(xs_rows[:], x_sample.rearrange("b s (c f) -> (b s c) f", f=P)).then_inc(xs_in, 16)
            for t in range(4):
                sp.dma_start(x_rows[:, t, :], x_prompt[0, t * P:(t + 1) * P, :]).then_inc(x_in[t], 16)

            def load(n, j, src, first=False):
                if not first:
                    sp.wait_ge(hi_ready, 8 * n + (j - 3))
                    sp.wait_ge(lo_ready, 8 * n + (j - 3))
                    sp.sem_inc(loads, 1)
                sp.dma_start(raw[:, j % RING, :].rearrange("p (k e) -> p k e", k=2), src).then_inc(raw_in[j % RING], 16)

            def load_heads(i):
                sp.dma_start(aux_raw[:, 0:256].rearrange("p (h e) -> p h e", h=2),
                             w_rg_a[0, bass.ds(2 * i, 2)].rearrange("h p e -> p h e")).then_inc(aux_in, 16)
                sp.dma_start(aux_raw[:, 256:512].rearrange("p (h e) -> p h e", h=2),
                             w_rg_x[0, bass.ds(2 * i, 2)].rearrange("h p e -> p h e")).then_inc(aux_in, 16)

            def heads_turn(i, first):
                for j in range(PAIR_UNITS):
                    load(2 * i, j, w_in_v[:, 2 * j:2 * j + 2, bass.ds(256 * i, 256)], first and j < RING)
                if first:
                    sp.wait_ge(small_t, 1)
                else:
                    sp.wait_ge(aux_hi, i)
                    sp.wait_ge(aux_lo, i)
                    sp.sem_inc(loads, 1)
                load_heads(i)
                for j in range(PAIR_UNITS):
                    load(2 * i + 1, j, w_in_v[:, 2 * j:2 * j + 2, bass.ds(W_LRU + 256 * i, 256)])

            heads_turn(0, True)
            with sp.Fori(1, 4) as i:
                heads_turn(i, False)
            with sp.Fori(0, 4) as n:
                for j in range(PAIR_UNITS):
                    load(8 + n, j, w_in_v[:, 2 * j:2 * j + 2, bass.ds(2 * W_LRU + 768 - 256 * n, 256)])
                sp.wait_ge(aux_hi, 4 + n)
                sp.wait_ge(aux_lo, 4 + n)
                sp.sem_inc(loads, 1)
                sp.dma_start(aux_raw[:].rearrange("p (k e) -> p k e", k=2),
                             w_pool[0, bass.ds(3 - n, 1)].rearrange("g (k p) e -> p (g k) e", p=P)).then_inc(aux_in, 16)
            with sp.Fori(0, OUT_PAIRS) as o:
                for j in range(PAIR_UNITS):
                    load(IN_PAIRS + o, j, w_out_v[:, y_row(2 * j):y_row(2 * j) + 2, bass.ds(256 * o, 256)])
            with sp.Fori(0, GROUPS) as g:
                with sp.Fori(0, MLP_PAIRS) as p:
                    for j in range(PAIR_UNITS):
                        load(20 + 16 * g + p, j, w_up_v[:, 2 * j:2 * j + 2, bass.ds(2048 * g + 256 * p, 256)])
                with sp.Fori(0, MLP_PAIRS) as p:
                    for j in range(PAIR_UNITS):
                        load(28 + 16 * g + p, j, w_down_v[:, bass.ds(16 * g + 2 * j, 2), bass.ds(256 * p, 256)])

            y_out = [y_prompt[0, t * P:(t + 1) * P, :] for t in range(4)] + [y_sample.rearrange("b s d -> (b s) d")]
            for m in range(20):
                t, c = m // 4, m % 4
                rows = P if t < 4 else SAMPLES
                sp.wait_ge(y_even if m % 2 == 0 else y_odd, m // 2 + 1)
                sp.dma_start(y_out[t][:, c * 512:(c + 1) * 512], raw[0:rows, m % RING, :]).then_inc(y_stored[m % RING], 16)
            for s in y_stored:
                sp.wait_ge(s, 16 * 5)

        @block.gpsimd
        def _(pool):
            pool.memset(ident[:], 0.0).then_inc(ident_ready, 1)
            pool.wait_ge(ident_ready, 1)
            pool.affine_select(out=ident[:], in_=ident[:], compare_op=ALU.not_equal, fill=1.0, base=0,
                               pattern=[[-1, P]], channel_multiplier=1).then_inc(ident_ready, 1)
            pool.dma_start(conv_sample[0, :, 0:2, :], state_conv[0, :, 1:3, :]).then_inc(states_stored, 16)
            pool.dma_start(pool_sample[0, :, 0:POOL_BUF - 1, :], state_pool[0, :, 1:POOL_BUF, :]).then_inc(states_stored, 16)
            for k in range(KC):
                pool.wait_ge(x_staged, k + 1)
                pool.dma_start(x_t_dram[k], scratch[:, k % 4, 0:PROMPT]).then_inc(spilled[k % 4], 16)
            pool.wait_ge(x_t, KC)
            pool.dma_start(state_rows[0:64, 0, :],
                           state_lru_h[0].rearrange("b (c f) -> (b c) f", f=P)).then_inc(states_in, 16)
            pool.dma_start(state_rows[0:96, 1:3, :],
                           state_conv[0].rearrange("(t b) k (c f) -> (b k c) t f", t=2, f=P)).then_inc(states_in, 16)
            pool.dma_start(state_rows[0:120, 3:11, :],
                           state_pool[0].rearrange("b k (c f) -> (k c) b f", f=P)).then_inc(states_in, 16)
            pool.wait_ge(pooled_lo, 4)
            pool.wait_ge(pooled_hi, 4)
            pool.wait_ge(last_ready, 1)
            for s in spilled:
                pool.wait_ge(s, 16 * 4)
            for c in range(4):
                pool.dma_start(resid[:, 4 * c:4 * c + 4, 0:PROMPT],
                               x_t_dram[4 * c:4 * c + 4].rearrange("k p t -> p k t")).then_inc(x_back, 16)
            pool.wait_ge(last_copied, 4)
            rows = aux_raw[:].rearrange("p (n f) -> p n f", n=4)
            pool.dma_start(lru_prompt[0, 0, :].rearrange("(c f) -> c f", f=P), rows[0:8, 0, :]).then_inc(states_stored, 16)
            pool.dma_start(lru_sample[0].rearrange("b (c f) -> (b c) f", f=P), rows[8:72, 0, :]).then_inc(states_stored, 16)
            pool.dma_start(conv_prompt[0, 0].rearrange("k (c f) -> (k c) f", f=P), rows[0:24, 1, :]).then_inc(states_stored, 16)
            for b in range(SAMPLES):
                pool.dma_start(conv_sample[0, b, 2, :].rearrange("(c f) -> c f", f=P),
                               rows[24 + 8 * b:32 + 8 * b, 1, :]).then_inc(states_stored, 16)
            pool.dma_start(pool_prompt[0, 0].rearrange("k (c f) -> (k c) f", f=P), rows[0:120, 2, :]).then_inc(states_stored, 16)
            for b in range(SAMPLES):
                pool.dma_start(pool_sample[0, b, POOL_BUF - 1, :].rearrange("(c f) -> c f", f=P),
                               rows[8 * b:8 * b + 8, 3, :]).then_inc(states_stored, 16)
            pool.wait_ge(states_stored, 16 * (6 + 2 * SAMPLES))

        @block.tensor
        def _(pe):
            def unit(n, j, buf, high, low):
                pe.wait_ge(hi_ready, 8 * n + (j + 1))
                pe.wait_ge(lo_ready, 8 * n + (j + 1))
                s = j % RING
                for kk in range(2):
                    k = 2 * j + kk
                    first, last = k == 0, k == KC - 1
                    for t in range(2):
                        wh, wl = (w[:, s, kk, t * P:(t + 1) * P] for w in (w_high, w_low))
                        for a in range(2):
                            out = ps[:, 4 * buf + 2 * t + a, 0:HALF]
                            pe.matmul(out, wh, high[:, k, a * HALF:(a + 1) * HALF], start=first, stop=False)
                        for a in range(2):
                            out = ps[:, 4 * buf + 2 * t + a, 0:HALF]
                            pe.matmul(out, wh, low[:, k, a * HALF:(a + 1) * HALF], start=False, stop=False)
                        for a in range(2):
                            out = ps[:, 4 * buf + 2 * t + a, 0:HALF]
                            mm = pe.matmul(out, wl, high[:, k, a * HALF:(a + 1) * HALF], start=False, stop=last)
                mm.then_inc(unit_used, 1)

            def split_product(banks, w_col, terms, done):
                for a in range(2):
                    out = ps[:, banks + a, 0:HALF]
                    for m, (slot, col) in enumerate(terms):
                        wh, wl = aux_high[:, col:col + P], aux_low[:, col:col + P]
                        xh = y_high[:, bass.ds(slot, 1), a * HALF:(a + 1) * HALF]
                        xl = y_low[:, bass.ds(slot, 1), a * HALF:(a + 1) * HALF]
                        pe.matmul(out, wh, xh, start=(m == 0), stop=False)
                        pe.matmul(out, wh, xl, start=False, stop=False)
                        mm = pe.matmul(out, wl, xh, start=False, stop=(m == len(terms) - 1))
                if done is not None:
                    mm.then_inc(done, 1)

            def gates(i, h):
                if h == 0:
                    pe.wait_ge(xc_hi, i + 1)
                    pe.wait_ge(xc_lo, i + 1)
                    pe.wait_ge(aux_hi, i + 1)
                    pe.wait_ge(aux_lo, i + 1)
                else:
                    pe.wait_ge(gates_tanh, 4 * i + 2)
                split_product(0, h * P, [(2 * i + h, h * P)], None)
                split_product(2, (2 + h) * P, [(2 * i + h, (2 + h) * P)], gates_mm)

            def pool_product(n):
                pe.wait_ge(pooled_hi, n + 1)
                pe.wait_ge(pooled_lo, n + 1)
                pe.wait_ge(aux_hi, 5 + n)
                pe.wait_ge(aux_lo, 5 + n)
                slots = (HEADS + 2 * n, HEADS + 2 * n + 1)
                for t in range(2):
                    split_product(4 * (n % 2) + 2 * t, None, [(slots[k], k * 256 + t * P) for k in range(2)],
                                  pool_mm if t == 1 else None)

            pe.wait_ge(ident_ready, 2)
            pe.wait_ge(vectors_in, 16 * 9)
            pe.transpose(ps[:, 4, 0:VECTORS], aux_raw[0:VECTORS, 0:P], ident[0:VECTORS, 0:VECTORS]).then_inc(small_t, 1)
            pe.wait_ge(xs_in, 16)
            pe.transpose(ps[:, 4, P:2 * P], xs_rows[:], ident[:]).then_inc(small_t, 1)
            for t in range(4):
                pe.wait_ge(x_in[t], 16)

            def turn_x(k):
                if k == 0:
                    pe.wait_ge(small_copied, 2)
                if k >= 4:
                    pe.wait_ge(x_hi, k - 3)
                for t in range(4):
                    mm = pe.transpose(ps[:, 4 + k % 4, t * P:(t + 1) * P], x_rows[:, t, k * P:(k + 1) * P], ident[:])
                mm.then_inc(x_t, 1)

            for k in range(4):
                turn_x(k)
            pe.wait_ge(sumsq_ready, 5)
            pe.wait_ge(xs_hi, 1)
            pe.wait_ge(xs_lo, 1)
            for j in range(PAIR_UNITS):
                for k in (2 * j + 4, 2 * j + 5):
                    if k < KC:
                        turn_x(k)
                pe.wait_ge(x_hi, 2 * j + 2)
                pe.wait_ge(x_lo, 2 * j + 2)
                unit(0, j, 0, h_high, h_low)
            pe.wait_ge(x_hi, KC)
            pe.wait_ge(vec_order, 1)
            pe.wait_ge(diag_ready, 5)
            pe.matmul(ps[:, 7, 0:256], ones[:], rstd[:, 0:256], start=True, stop=True)
            pe.matmul(ps[:, 7, 256:512], ones[:], rstd[:, 256:512], start=True, stop=True)
            pe.matmul(ps[:, 4, 504:512], ones[:], rstd[:, 512:520], start=True, stop=True).then_inc(total_ready, 1)
            pe.wait_ge(states_in, 48)
            pe.transpose(ps[:, 4, 0:64], state_rows[0:64, 0, :], ident[0:64, 0:64])
            for t in range(2):
                pe.transpose(ps[:, 4, 64 + 96 * t:160 + 96 * t], state_rows[0:96, 1 + t, :], ident[0:96, 0:96])
            for b in range(SAMPLES):
                mm = pe.transpose(ps[:, 5 + b // 4, 120 * (b % 4):120 * (b % 4) + 120], state_rows[0:120, 3 + b, :],
                                  ident[0:120, 0:120])
            mm.then_inc(states_t, 1)

            def gate_pair(i, first):
                if first:
                    pe.wait_ge(states_copied, 2)
                    pe.wait_ge(mean_ready, 1)
                else:
                    pe.wait_ge(gate_evac, 2 * i)
                for j in range(PAIR_UNITS):
                    unit(2 * i + 1, j, 1, h_high, h_low)
                    if j == 4:
                        gates(i, 0)
                    if j == 6:
                        gates(i, 1)

            gate_pair(0, True)
            with pe.Fori(1, 4) as i:
                pe.wait_ge(gates_tanh, 4 * i)
                for j in range(PAIR_UNITS):
                    unit(2 * i, j, 0, h_high, h_low)
                gate_pair(i, False)

            for n in range(4):
                if n == 0:
                    pe.wait_ge(gates_tanh, 16)
                elif n == 1:
                    pe.wait_ge(gate_evac, 8)
                else:
                    pe.wait_ge(pair_evac, n - 1)
                for j in range(PAIR_UNITS):
                    unit(8 + n, j, n % 2, h_high, h_low)
                    if n >= 1 and j == 6:
                        pool_product(n - 1)

            def out_unit(o, j, buf):
                unit(IN_PAIRS + o, j, buf, y_high, y_low)

            pe.wait_ge(pair_evac, 3)
            pe.wait_ge(y_hi, 4)
            pe.wait_ge(y_lo, 4)
            for j in range(PAIR_UNITS):
                if j >= 4:
                    pe.wait_ge(y_hi, 4 + 2 * (j - 3))
                    pe.wait_ge(y_lo, 4 + 2 * (j - 3))
                out_unit(0, j, 0)
                if j == 3:
                    pool_product(3)
            pe.wait_ge(pair_evac, 4)
            pe.wait_ge(last_ready, 1)
            for m, (rows, last) in enumerate(((72, lru_last[:]), (88, conv_last[:]), (120, pool_last[:, 0:POOL_BUF, :]),
                                              (64, pool_last[:, POOL_BUF:POOL_BUF + SAMPLES, :]))):
                pe.transpose(ps[0:rows, 4 + m, 0:P], last.rearrange("p j c -> p (j c)"), ident[:]).then_inc(last_t, 1)
            pe.wait_ge(last_copied, 4)
            for j in range(PAIR_UNITS):
                out_unit(1, j, 1)
            with pe.Fori(1, OUT_PAIRS // 2) as b:
                for half in range(2):
                    pe.wait_ge(pair_evac, 2 * b + (half + 3))
                    for j in range(PAIR_UNITS):
                        out_unit(2 * b + half, j, half)

            pe.wait_ge(sq_summed, OUT_PAIRS)
            pe.wait_ge(pair_evac, 12)
            for a in range(2):
                for t in range(2):
                    mm = pe.matmul(ps[:, 4 + a, 0:HALF], ones[:], scratch[:, 2 + t, a * HALF:(a + 1) * HALF],
                                   start=(t == 0), stop=(t == 1))
            mm.then_inc(total_ready, 1)
            pe.wait_ge(mean_ready, 2)
            with pe.Fori(0, GROUPS) as g:
                with pe.Fori(0, MLP_PAIRS // 2) as b:
                    for half in range(2):
                        pe.wait_ge(pair_evac, 16 * g + 2 * b + (half + 11))
                        for j in range(PAIR_UNITS):
                            if half == 0:
                                pe.wait_ge(h2_hi, 2 * j + 2)
                                pe.wait_ge(h2_lo, 2 * j + 2)
                            unit(16 * g + 2 * b + (20 + half), j, half, h_high, h_low)
                with pe.Fori(0, MLP_PAIRS // 2) as b:
                    for half in range(2):
                        pe.wait_ge(pair_evac, 16 * g + 2 * b + (half + 19))
                        for j in range(PAIR_UNITS):
                            if half == 0:
                                pe.wait_ge(f_hi, 8 * g + (j + 1))
                                pe.wait_ge(f_lo, 8 * g + (j + 1))
                            unit(16 * g + 2 * b + (28 + half), j, half, y_high, y_low)

            pe.wait_ge(final_sq, OUT_PAIRS)
            for t in range(5):
                rows = P if t < 4 else SAMPLES
                for a in range(2):
                    mm = pe.matmul(ps[0:rows, 0, t:t + 1], scratch[:, 2 + a, t * P:t * P + rows], ones[:, 0:1],
                                   start=(a == 0), stop=(a == 1))
            mm.then_inc(final_total, 1)
            pe.wait_ge(final_scaled, OUT_PAIRS)
            for m in range(20):
                t, c = m // 4, m % 4
                rows = P if t < 4 else SAMPLES
                if m >= 7:
                    pe.wait_ge(y_even if (m - 7) % 2 == 0 else y_odd, (m - 7) // 2 + 1)
                for f in range(4):
                    mm = pe.transpose(ps[0:rows, 1 + m % 7, f * P:(f + 1) * P], resid[:, 4 * c + f, t * P:t * P + rows],
                                      ident[:])
                mm.then_inc(y_t, 1)

        @block.scalar
        def _(act):
            order = Order(act, act_order)

            def convert(n, j, first=False):
                act.wait_ge(raw_in[j % RING], 32 * n + 16 * (j // RING + 1))
                if not first:
                    act.wait_ge(unit_used, 8 * n + (j - 3))
                act.activation(w_high[:, j % RING].rearrange("p k e -> p (k e)"), raw[:, j % RING, :],
                               ACT.Copy).then_inc(hi_ready, 1)

            def convert_aux(m, landed, user, used):
                act.wait_ge(aux_in, landed)
                if user is not None:
                    act.wait_ge(user, used)
                act.activation(aux_high[:], aux_raw[:], ACT.Copy).then_inc(aux_hi, 1)

            def root(m):
                act.wait_ge(mean_ready, m)
                act.activation(scratch[:, 1, :], scratch[:, 0, :], ACT.Sqrt).then_inc(root_ready, 1)

            junk = ps[:, 0:4, :].rearrange("p b t -> p (b t)")
            act.wait_ge(xs_in, 16)
            act.activation(junk[:, 0:P], xs_rows[:], ACT.Square, accum_out=sumsq[:, 4:5]).then_inc(sumsq_ready, 1)
            for t in range(4):
                act.wait_ge(x_in[t], 16)
                act.wait_ge(sumsq_ready, t + 1)
                act.activation(junk, x_rows[:, t, :], ACT.Square, accum_out=sumsq[:, t:t + 1]).then_inc(sumsq_ready, 1)
            act.wait_ge(small_copied, 2)
            act.wait_ge(xs_scaled, 1)
            act.activation(h_high[:, :, PROMPT:TOK], rstd[:, 0:P].rearrange("p (c b) -> p c b", b=SAMPLES),
                           ACT.Copy).then_inc(xs_hi, 1)

            def heads_tail(i, j):
                if j == 2:
                    gate_activations(i, 1)
                if j == 4:
                    act.wait_ge(tanh_used, i + 1)
                    act.activation(tanh_a, tanh_a, ACT.Sqrt).then_inc(root_t, 1)
                    act.wait_ge(gate_evac, 2 * i + 2)
                    act.wait_ge(xi_ready, i + 1)
                    act.activation(tanh_x, gate, ACT.Square).then_inc(gate_sq, 1)
                if j == 8:
                    act.wait_ge(gate_arg, i + 1)
                    act.activation(tanh_x, tanh_x, ACT.Tanh, scale=SQRT_2_OVER_PI).then_inc(gate_th, 1)
                if j == 9:
                    act.wait_ge(lru_y, i + 1)
                    act.activation(y_high[:, bass.ds(2 * i, 2), :], gate, ACT.Copy).then_inc(y_hi, 1)

            def gate_activations(i, h):
                act.wait_ge(gates_mm, 2 * i + (h + 1))
                act.activation(halves(tanh_a[:, h]), bank(0, 0), ACT.Tanh, scale=0.5,
                               bias=half_bias[:, bass.ds(2 * i + h, 1)]).then_inc(gates_tanh, 1)
                act.activation(halves(tanh_x[:, h]), bank(0, 1), ACT.Tanh, scale=0.5,
                               bias=half_bias[:, bass.ds(2 * i + h + HEADS, 1)]).then_inc(gates_tanh, 1)
                act.wait_ge(gates_tanh, 4 * i + (2 * h + 1))
                act.activation(q[:, h], tanh_a[:, h], ACT.Exp, scale=lru_c[:, 1, bass.ds(2 * i + h, 1)],
                               bias=lru_c[:, 1, bass.ds(2 * i + h, 1)]).then_inc(decay_exp, 1)
                act.activation(tanh_a[:, h], tanh_a[:, h], ACT.Tanh, scale=lru_c[:, 0, bass.ds(2 * i + h, 1)],
                               bias=lru_c[:, 0, bass.ds(2 * i + h, 1)]).then_inc(decay_tanh, 1)

            def gate_slot(i, j):
                if j == 0:
                    convert_aux(i, 32 * i + 32, None if isinstance(i, int) else gates_mm, 2 * i)
                if j == 4:
                    for h in range(2):
                        if h == 0:
                            act.wait_ge(ext_ready, i + 1)
                        act.activation(conv_sum[:, h], conv_in[:, h, 0:CONV], ACT.Identity,
                                       scale=column("conv_w", 2 * i + h),
                                       bias=column("conv_b", 2 * i + h)).then_inc(tap0_ready, 1)
                if j == 6:
                    act.wait_ge(xc_ready, i + 1)
                    act.activation(y_high[:, bass.ds(2 * i, 2), :], xc, ACT.Copy).then_inc(xc_hi, 1)
                if j == 7:
                    gate_activations(i, 0)

            for j in range(PAIR_UNITS):
                convert(0, j, j < RING)
                for k in (2 * j, 2 * j + 1):
                    act.wait_ge(x_t, k + 1)
                    if k >= 4:
                        act.wait_ge(spilled[k % 4], 16 * (k // 4))
                        act.wait_ge(x_lo, k - 3)
                    act.activation(scratch[:, k % 4, 0:PROMPT], ps[:, 4 + k % 4, :], ACT.Copy).then_inc(x_staged, 1)
                    act.activation(h_high[:, k, 0:PROMPT], ps[:, 4 + k % 4, :], ACT.Copy,
                                   scale=column("g_mix", k)).then_inc(x_hi, 1)
            for j in range(PAIR_UNITS):
                convert(1, j)
                if j == 1:
                    act.wait_ge(lam_ready, 1)
                    act.activation(tiny[:, 1, :], tiny[:, 0, :], ACT.Tanh, scale=1.0 / 32.0).then_inc(lam_tanh, 1)
                if j == 2:
                    root(1)
                gate_slot(0, j)
            with act.Fori(1, 4) as i:
                for j in range(PAIR_UNITS):
                    convert(2 * i, j)
                    heads_tail(i - 1, j)
                for j in range(PAIR_UNITS):
                    convert(2 * i + 1, j)
                    heads_tail(i - 1, PAIR_UNITS + j)
                    gate_slot(i, j)

            def pool_result(n):
                act.wait_ge(pool_mm, n + 1)
                for t in range(2):
                    act.activation(halves(y_high[:, HEADS + 2 * n + t, :]), bank(n % 2, t), ACT.Copy,
                                   scale=column("pool_scale", 2 * pool_group(n) + t)).then_inc(y_hi, 1)

            def pool_slot(n, j):
                if j == 2 and n >= 2:
                    pool_result(n - 2)
                if j == 2 and n >= 1:
                    convert_aux(3 + n, 128 + 16 * n, pool_mm if n >= 2 else gates_mm, n - 1 if n >= 2 else 8)
                if j == 6 and n >= 1:
                    act.wait_ge(pooled_ready, n)
                    act.activation(y_high[:, HEADS + 2 * n - 2:HEADS + 2 * n, :], pooled, ACT.Copy).then_inc(pooled_hi, 1)

            for n in range(4):
                for j in range(PAIR_UNITS):
                    convert(8 + n, j)
                    if n < 2:
                        heads_tail(3, PAIR_UNITS * n + j)
                    pool_slot(n, j)

            def out_steps(o):
                act.wait_ge(pair_evac, o + 5)
                for t in range(2):
                    act.activation(h_high[:, bass.ds(2 * o + t, 1), :].rearrange("p k t -> p (k t)"),
                                   resid[:, bass.ds(2 * o + t, 1), :].rearrange("p k t -> p (k t)"), ACT.Copy,
                                   scale=column("g_mlp", 2 * o + t)).then_inc(h2_hi, 1)
                if isinstance(o, int) and o == 0:
                    act.wait_ge(spilled[3], 64)
                    act.activation(scratch[:, 2:4, :], resid[:, 0:2, :], ACT.Square).then_inc(out_sq, 1)
                else:
                    act.wait_ge(sq_summed, 1)
                    act.wait_ge(sq_summed, o)
                    act.activation(scratch[:, 0:2, :], resid[:, bass.ds(2 * o, 2), :], ACT.Square).then_inc(out_sq, 1)

            for n in range(2):
                for j in range(PAIR_UNITS):
                    convert(IN_PAIRS + n, j)
                    if n == 0:
                        pool_slot(4, j)
                        if j == 7:
                            pool_result(3)
                    elif j == 4:
                        out_steps(0)
            with act.Fori(1, OUT_PAIRS // 2) as b:
                for half in range(2):
                    for j in range(PAIR_UNITS):
                        convert(2 * b + (IN_PAIRS + half), j)
                        if j == 4:
                            out_steps(2 * b + (half - 1))

            def up_steps(m):
                act.wait_ge(f_relu, 2 * m + 2)
                act.activation(scratch[:, 0:2, :], scratch[:, 0:2, :], ACT.Square).then_inc(f_sq, 1)
                act.wait_ge(f_sq, m + 1)

            def up_high(m, p):
                act.activation(y_high[:, bass.ds(2 * p, 2), :], scratch[:, 0:2, :], ACT.Copy).then_inc(f_hi, 1)

            def final_steps(p):
                act.wait_ge(pair_evac, 69 + p)
                if p == 0:
                    act.activation(scratch[:, 2:4, :], resid[:, 0:2, :], ACT.Square).then_inc(out_sq, 1)
                    act.wait_ge(out_sq, OUT_PAIRS + 1)
                else:
                    act.wait_ge(final_sq, p)
                    act.activation(scratch[:, 0:2, :], resid[:, 2 * p:2 * p + 2, :], ACT.Square).then_inc(out_sq, 1)
                    act.wait_ge(out_sq, OUT_PAIRS + 1 + p)
                for t in range(2):
                    k = 2 * p + t
                    ins = act.activation(resid[:, k, :], resid[:, k, :], ACT.Copy, scale=column("g_final", k))
                ins.then_inc(final_scaled, 1)

            def quarter(g, head, last):
                for j in range(PAIR_UNITS):
                    convert(16 * g + 20, j)
                    if j == 3 and head == "out":
                        out_steps(OUT_PAIRS - 1)
                        root(2)
                for j in range(PAIR_UNITS):
                    convert(16 * g + 21, j)
                    if j == 4:
                        up_steps(8 * g)
                        up_high(8 * g, 0)
                with act.Fori(1, MLP_PAIRS // 2) as b:
                    for half in range(2):
                        for j in range(PAIR_UNITS):
                            convert(16 * g + 2 * b + (20 + half), j)
                            if j == 4:
                                up_steps(8 * g + 2 * b + (half - 1))
                                up_high(8 * g + 2 * b + (half - 1), 2 * b + (half - 1))
                for j in range(PAIR_UNITS):
                    convert(16 * g + 28, j)
                    if j == 3:
                        up_steps(8 * g + 7)
                        up_high(8 * g + 7, 7)
                if not last:
                    with act.Fori(1, MLP_PAIRS) as p:
                        for j in range(PAIR_UNITS):
                            convert(16 * g + p + 28, j)
                else:
                    for p in range(1, MLP_PAIRS):
                        for j in range(PAIR_UNITS):
                            convert(16 * g + p + 28, j)
                            if j == 4:
                                final_steps(p - 1)

            quarter(0, "out", False)
            with act.Fori(1, GROUPS - 1) as g:
                quarter(g, "down", False)
            quarter(GROUPS - 1, "down", True)
            final_steps(MLP_PAIRS - 1)
            act.wait_ge(final_rstd, 1)
            act.activation(r_final[:, 1, :], r_final[:, 0, :], ACT.Sqrt).then_inc(root_ready, 1)
            act.wait_ge(final_rstd, 2)
            for m in range(0, 20, 2):
                t, rows = m // 4, P if m < 16 else SAMPLES
                act.wait_ge(y_t, m + 1)
                if m >= RING:
                    act.wait_ge(y_stored[m % RING], 16 * (m // RING))
                act.activation(raw[0:rows, m % RING, :], ps[0:rows, 1 + m % 7, :], ACT.Copy,
                               scale=r_final[0:rows, 3, t:t + 1]).then_inc(y_even, 1)

        @block.vector
        def _(dve):
            order = Order(dve, vec_order)
            step = order.mark
            settle = order.settle

            def convert(n, j, first=False):
                dve.wait_ge(hi_ready, 8 * n + (j + 1))
                if not first:
                    dve.wait_ge(unit_used, 8 * n + (j - 3))
                s = j % RING
                dve.tensor_tensor(w_low[:, s].rearrange("p k e -> p (k e)"), raw[:, s, :],
                                  w_high[:, s].rearrange("p k e -> p (k e)").bitcast(F32),
                                  ALU.subtract).then_inc(lo_ready, 1)

            def convert_aux(m):
                dve.wait_ge(aux_hi, m + 1)
                dve.tensor_tensor(aux_low[:], aux_raw[:], aux_high[:].bitcast(F32), ALU.subtract).then_inc(aux_lo, 1)

            def newton(y, v, t, root):
                step(dve.reciprocal(y, root))
                settle()
                step(dve.tensor_tensor(t, y, y, ALU.mult))
                settle()
                step(dve.tensor_tensor(t, t, v, ALU.mult))
                settle()
                step(dve.tensor_scalar(t, t, -0.5, 1.5, ALU.mult, ALU.add))
                settle()
                return dve.tensor_tensor(y, y, t, ALU.mult)

            step(dve.memset(ones[:], 1.0))
            step(dve.memset(r_final[:], 1.0))
            for c in range(POOL_BUF):
                step(dve.memset(inv_count[:, c:c + 1], 1.0 / (c + 1)))
            dve.wait_ge(small_t, 2)
            dve.tensor_copy(vec[:, 0:VECTORS], ps[:, 4, 0:VECTORS]).then_inc(small_copied, 1)
            dve.tensor_copy(xs_t[:], ps[:, 4, P:2 * P]).then_inc(small_copied, 1)
            dve.wait_ge(small_copied, 2)
            xs_g = rstd[:, 0:P].rearrange("p (c b) -> p c b", b=SAMPLES)
            dve.tensor_tensor(xs_g, xs_t[:].rearrange("p (b c) -> p c b", b=SAMPLES),
                              vec[:, 0:KC].unsqueeze(2).broadcast_to([P, KC, SAMPLES]), ALU.mult).then_inc(xs_scaled, 1)
            dve.wait_ge(xs_hi, 1)
            dve.tensor_tensor(h_low[:, :, PROMPT:TOK], xs_g, h_high[:, :, PROMPT:TOK].bitcast(F32),
                              ALU.subtract).then_inc(xs_lo, 1)
            dve.wait_ge(xs_lo, 1)

            def heads_tail(i, j):
                if j == 2:
                    dve.wait_ge(gates_tanh, 4 * i + 4)
                    dve.scalar_tensor_tensor(out=xc, in0=tanh_x, scalar=1.0, in1=xc, op0=ALU.add,
                                             op1=ALU.mult).then_inc(xi_ready, 1)
                    dve.wait_ge(decay_exp, 2 * i + 2)
                    step(dve.tensor_scalar(q, q, 0.5, 0.5, ALU.mult, ALU.add))
                if j == 3:
                    dve.wait_ge(unit_used, 16 * i + 16)
                    for h in range(2):
                        dve.tensor_tensor(halves(gate[:, h]), bank(1, h), halves(rstd[:]), ALU.mult).then_inc(gate_evac, 1)
                if j == 4:
                    settle()
                    dve.wait_ge(decay_tanh, 2 * i + 2)
                    dve.scalar_tensor_tensor(out=decay, in0=tanh_a, scalar=1.0, in1=q, op0=ALU.add,
                                             op1=ALU.mult).then_inc(tanh_used, 1)
                    dve.wait_ge(tanh_used, i + 1)
                    step(dve.tensor_scalar(decay, decay, -1.0, 2.0, ALU.mult, ALU.add))
                    settle()
                    step(dve.tensor_tensor(q, q, decay, ALU.mult))
                if j == 5:
                    settle()
                    step(dve.tensor_scalar(decay, q, 2.0, -1.0, ALU.mult, ALU.add))
                    dve.wait_ge(root_t, i + 1)
                    step(dve.tensor_tensor(q, tanh_a, q, ALU.mult))
                    settle()
                    step(dve.memset(q[:, :, 0:1], 0.5))
                if j == 6:
                    settle()
                    dve.wait_ge(xi_ready, i + 1)
                    step(dve.tensor_tensor(xc, xc, q, ALU.mult))
                    dve.wait_ge(gate_sq, i + 1)
                    step(dve.tensor_scalar(tanh_x, tanh_x, GELU_CUBIC, 1.0, ALU.mult, ALU.add))
                    settle()
                    dve.tensor_tensor(tanh_x, tanh_x, gate, ALU.mult).then_inc(gate_arg, 1)
                if j == 7:
                    for h in range(2):
                        step(dve.tensor_tensor_scan(tanh_a[:, h, 0:PROMPT], decay[:, h, 0:PROMPT], xc[:, h, 0:PROMPT],
                                                    0.0, ALU.mult, ALU.add))
                    h0 = states[:, 0:64].rearrange("p (b c) -> p c b", b=SAMPLES)[:, bass.ds(2 * i, 2), :]
                    step(dve.tensor_tensor(tanh_a[:, :, PROMPT:TOK], decay[:, :, PROMPT:TOK], h0, ALU.mult))
                    settle()
                    step(dve.tensor_tensor(tanh_a[:, :, PROMPT:TOK], tanh_a[:, :, PROMPT:TOK], xc[:, :, PROMPT:TOK], ALU.add))
                    settle()
                    step(dve.tensor_copy(lru_last[:].rearrange("p j c -> p c j")[:, bass.ds(2 * i, 2), :],
                                         tanh_a[:, :, PROMPT - 1:TOK]))
                if j == 8:
                    dve.wait_ge(gate_th, i + 1)
                    step(dve.scalar_tensor_tensor(out=gate, in0=tanh_x, scalar=1.0, in1=gate, op0=ALU.add, op1=ALU.mult))
                    settle()
                    dve.scalar_tensor_tensor(out=gate, in0=tanh_a, scalar=0.5, in1=gate, op0=ALU.mult,
                                             op1=ALU.mult).then_inc(lru_y, 1)
                if j == 9:
                    dve.wait_ge(y_hi, i + 1)
                    dve.tensor_tensor(y_low[:, bass.ds(2 * i, 2), :], gate, y_high[:, bass.ds(2 * i, 2), :].bitcast(F32),
                                      ALU.subtract).then_inc(y_lo, 1)

            TAIL_STEPS = 14

            def gate_slot(i, j):
                if j == 0:
                    convert_aux(i)
                if j == 3:
                    step(dve.memset(conv_in[:, :, 0:3], 0.0))
                    for h in range(2):
                        old = states[:, ST_CONV:ST_POOL].rearrange("p (b k c) -> p c b k", b=SAMPLES, k=3)
                        new = conv_in[:, h, EXT_S:EXT_S + CONV_W * SAMPLES].rearrange("p (b k) -> p b k", k=CONV_W)
                        step(dve.tensor_copy(new[:, :, 0:3].unsqueeze(1), old[:, bass.ds(2 * i + h, 1)]))
                    dve.wait_ge(unit_used, 16 * i + 8)
                    for h in range(2):
                        step(dve.tensor_tensor(halves(conv_in[:, h, 3:3 + TOK]), bank(0, h), halves(rstd[:]), ALU.mult))
                    settle()
                    ext = conv_in[:, :, EXT_S:EXT_S + CONV_W * SAMPLES].rearrange("p h (b k) -> p h b k", k=CONV_W)
                    dve.tensor_copy(ext[:, :, :, 3], conv_in[:, :, 3 + PROMPT:3 + TOK]).then_inc(ext_ready, 1)
                if j == 4:
                    for k in range(1, 3):
                        for h in range(2):
                            if k == 1:
                                dve.wait_ge(ext_ready, i + 1)
                                dve.wait_ge(tap0_ready, 2 * i + (h + 1))
                            step(dve.scalar_tensor_tensor(out=conv_sum[:, h], in0=conv_in[:, h, k:k + CONV],
                                                          scalar=column("conv_w", 2 * i + h + k * HEADS),
                                                          in1=conv_sum[:, h], op0=ALU.mult, op1=ALU.add))
                        settle()
                if j == 5:
                    for h in range(2):
                        w3 = column("conv_w", 2 * i + h + 3 * HEADS)
                        step(dve.scalar_tensor_tensor(out=xc[:, h, 0:PROMPT], in0=conv_in[:, h, 3:3 + PROMPT], scalar=w3,
                                                      in1=conv_sum[:, h, 0:PROMPT], op0=ALU.mult, op1=ALU.add))
                        ins = dve.scalar_tensor_tensor(
                            out=xc[:, h, PROMPT:TOK], in0=conv_in[:, h, 3 + PROMPT:3 + TOK], scalar=w3,
                            in1=conv_sum[:, h, EXT_S:EXT_S + CONV_W * (SAMPLES - 1) + 1:CONV_W],
                            op0=ALU.mult, op1=ALU.add)
                        if h == 0:
                            step(ins)
                    ins.then_inc(xc_ready, 1)
                if j == 6:
                    step(dve.tensor_copy(conv_last[:].rearrange("p j c -> p c j")[:, bass.ds(2 * i, 2), :],
                                         conv_in[:, :, PROMPT:3 + TOK]))
                    settle()
                    dve.wait_ge(xc_hi, i + 1)
                    dve.tensor_tensor(y_low[:, bass.ds(2 * i, 2), :], xc, y_high[:, bass.ds(2 * i, 2), :].bitcast(F32),
                                      ALU.subtract).then_inc(xc_lo, 1)

            GATE_STEPS = 5 + 4 + 3 + 1

            for j in range(PAIR_UNITS):
                convert(0, j, j < RING)
                if j == 0:
                    dve.wait_ge(sumsq_ready, 5)
                    dve.wait_ge(ident_ready, 2)
                    step(dve.tensor_reduce(sel[:], ident[:].rearrange("p (b c) -> p b c", b=SAMPLES), AX_X, ALU.add))
                    for t in range(4):
                        dve.tensor_scalar(rstd[:, t * P:(t + 1) * P], ident[:], sumsq[:, t:t + 1], None,
                                          ALU.mult).then_inc(diag_ready, 1)
                    settle()
                    dve.tensor_scalar(rstd[:, PROMPT:TOK], sel[:], sumsq[:, 4:5], None, ALU.mult).then_inc(diag_ready, 1)
                for k in (2 * j, 2 * j + 1):
                    dve.wait_ge(x_hi, k + 1)
                    dve.scalar_tensor_tensor(out=h_low[:, k, 0:PROMPT], in0=scratch[:, k % 4, 0:PROMPT],
                                             scalar=column("g_mix", k),
                                             in1=h_high[:, k, 0:PROMPT].bitcast(F32), op0=ALU.mult,
                                             op1=ALU.subtract).then_inc(x_lo, 1)
            for j in range(PAIR_UNITS):
                convert(1, j)
                if j == 0:
                    lam = vec[:, ROWS_OF["lam"]:ROWS_OF["lam"] + HEADS]
                    b = ROWS_OF["b_a"]
                    step(dve.tensor_scalar(half_bias[:], vec[:, b:b + 2 * HEADS], 0.5, None, ALU.mult))
                    dve.scalar_tensor_tensor(out=tiny[:, 0, :], in0=lam, scalar=-1.0, in1=lam, op0=ALU.mult,
                                             op1=ALU.max).then_inc(lam_ready, 1)
                if j == 1:
                    dve.wait_ge(lam_tanh, 1)
                    t, e, s, p = (tiny[:, m, :] for m in (1, 0, 2, 3))
                    step(dve.tensor_scalar(s, t, 1.0, None, ALU.add))
                    settle()
                    step(dve.reciprocal(p, s))
                    step(dve.tensor_scalar(e, t, -1.0, 1.0, ALU.mult, ALU.add))
                    settle()
                    step(dve.tensor_tensor(e, e, p, ALU.mult))
                    settle()
                    for _ in range(4):
                        step(dve.tensor_tensor(e, e, e, ALU.mult))
                        settle()
                    step(dve.tensor_scalar(s, e, 2.0, None, ALU.add))
                    settle()
                    step(dve.reciprocal(p, s))
                    settle()
                    step(dve.tensor_tensor(s, e, p, ALU.mult))
                    settle()
                    step(dve.tensor_tensor(t, s, s, ALU.mult))
                    settle()
                    step(dve.tensor_scalar(p, t, 1.0 / 17.0, None, ALU.mult))
                    settle()
                    for odd in (15, 13, 11, 9, 7, 5, 3):
                        step(dve.scalar_tensor_tensor(out=p, in0=p, scalar=1.0 / odd, in1=t, op0=ALU.add, op1=ALU.mult))
                        settle()
                    step(dve.scalar_tensor_tensor(out=s, in0=p, scalar=1.0, in1=s, op0=ALU.add, op1=ALU.mult))
                    step(dve.tensor_scalar(e, lam, -1.0, 0.0, ALU.mult, ALU.max))
                    settle()
                    step(dve.scalar_tensor_tensor(out=e, in0=s, scalar=2.0, in1=e, op0=ALU.mult, op1=ALU.add))
                    settle()
                    step(dve.tensor_scalar(lru_c[:, 0, :], e, 2.0, None, ALU.mult))
                    step(dve.tensor_scalar(lru_c[:, 1, :], e, -4.0, None, ALU.mult))
                if j == 2:
                    for s in spilled:
                        dve.wait_ge(s, 64)
                    dve.wait_ge(total_ready, 1)
                    dve.wait_ge(states_t, 1)
                    step(dve.tensor_scalar(scratch[:, 0, 0:PROMPT], ps[:, 7, :], 1.0 / D, EPS, ALU.mult, ALU.add))
                    dve.tensor_scalar(scratch[:, 0, PROMPT:TOK], ps[:, 4, 504:512], 1.0 / D, EPS, ALU.mult,
                                      ALU.add).then_inc(mean_ready, 1)
                    dve.tensor_copy(states[:, 0:ST_POOL], ps[:, 4, 0:ST_POOL]).then_inc(states_copied, 1)
                    dve.tensor_copy(states[:, ST_POOL:ST_COLS].rearrange("p (b t) -> p b t", b=2),
                                    ps[:, 5:7, 0:480]).then_inc(states_copied, 1)
                    dve.wait_ge(states_copied, 2)
                    dve.wait_ge(mean_ready, 1)
                    dve.wait_ge(root_ready, 1)
                    settle()
                    step(newton(rstd[:], scratch[:, 0, :], scratch[:, 1, :], scratch[:, 1, :]))
                    settle()
                gate_slot(0, j)
            with dve.Fori(1, 4) as i:
                order.enter(i - 1, TAIL_STEPS + GATE_STEPS)
                for j in range(PAIR_UNITS):
                    convert(2 * i, j)
                    heads_tail(i - 1, j)
                for j in range(PAIR_UNITS):
                    convert(2 * i + 1, j)
                    heads_tail(i - 1, PAIR_UNITS + j)
                    gate_slot(i, j)
                order.leave(3)

            def pool_result(n):
                for t in range(2):
                    dve.wait_ge(y_hi, 4 + 2 * n + t + 1)
                    y = HEADS + 2 * n + t
                    ins = dve.scalar_tensor_tensor(out=halves(y_low[:, y, :]), in0=bank(n % 2, t),
                                                   scalar=column("pool_scale", 2 * pool_group(n) + t),
                                                   in1=halves(y_high[:, y, :]).bitcast(F32), op0=ALU.mult, op1=ALU.subtract)
                    ins.then_inc(y_lo, 1)
                dve.wait_ge(y_lo, 4 + 2 * n + 2)
                dve.memset(sel[:, 0:1], 0.0).then_inc(pair_evac, 1)

            def pool_steps(n, j):
                g = pool_group(n)
                w = WINDOWS[g]
                ext = pool_in[:, :, PEXT_S:PEXT].rearrange("p t (b k) -> p t b k", k=POOL_BUF + 1)
                if j == 3:
                    if n == 0:
                        dve.wait_ge(y_lo, 4)
                    else:
                        dve.wait_ge(pooled_lo, n)
                        dve.wait_ge(pooled_ready, n)
                    settle()
                    step(dve.memset(pool_in[:, :, 0:POOL_BUF], 0.0))
                    for t in range(2):
                        old = states[:, ST_POOL:ST_COLS].rearrange("p (b k c) -> p c b k", b=SAMPLES, k=POOL_BUF)
                        step(dve.tensor_copy(ext[:, t, :, 0:POOL_BUF], old[:, 2 * g + t]))
                    dve.wait_ge(unit_used, 8 * (9 + n))
                    for t in range(2):
                        step(dve.tensor_tensor(halves(pool_in[:, t, POOL_BUF:POOL_BUF + TOK]), bank(n % 2, t), halves(rstd[:]),
                                               ALU.mult))
                    settle()
                    step(dve.tensor_copy(ext[:, :, :, POOL_BUF], pool_in[:, :, POOL_BUF + PROMPT:POOL_BUF + TOK]))
                    settle()
                    step(dve.tensor_copy(pool_last[:].rearrange("p j c -> p c j")[:, 2 * g:2 * g + 2, :],
                                         pool_in[:, :, PROMPT:POOL_BUF + TOK]))
                    src, dst, other, width = pool_in, sum_a, sum_b, 1
                    while width < w:
                        cols = PEXT - 2 * width + 1
                        step(dve.tensor_tensor(dst[:, :, 0:cols], src[:, :, 0:cols], src[:, :, width:width + cols], ALU.add))
                        settle()
                        src, dst, other, width = dst, other, dst, 2 * width
                    pool_steps.sums = src
                if j == 5:
                    sums = pool_steps.sums
                    start = POOL_BUF + 1 - w
                    sum_ext = sums[:, :, PEXT_S:PEXT].rearrange("p t (b k) -> p t b k", k=POOL_BUF + 1)
                    if n >= 1:
                        dve.wait_ge(pooled_hi, n)
                    step(dve.scalar_tensor_tensor(out=pooled[:, :, 0:PROMPT], in0=sums[:, :, start:start + PROMPT],
                                                  scalar=1.0 / w, in1=pool_in[:, :, POOL_BUF:POOL_BUF + PROMPT],
                                                  op0=ALU.mult, op1=ALU.subtract))
                    step(dve.scalar_tensor_tensor(out=pooled[:, :, PROMPT:TOK], in0=sum_ext[:, :, :, start], scalar=1.0 / w,
                                                  in1=pool_in[:, :, POOL_BUF + PROMPT:POOL_BUF + TOK],
                                                  op0=ALU.mult, op1=ALU.subtract))
                    for t in range(2):
                        step(dve.tensor_tensor(head_fix[:, t, 0:w - 1], sums[:, t, start:start + w - 1],
                                               inv_count[:, 0:w - 1], ALU.mult))
                    settle()
                    dve.tensor_tensor(pooled[:, :, 0:w - 1], head_fix[:, :, 0:w - 1],
                                      pool_in[:, :, POOL_BUF:POOL_BUF + w - 1], ALU.subtract).then_inc(pooled_ready, 1)
                if j == 6:
                    y = HEADS + 2 * n
                    dve.wait_ge(pooled_hi, n + 1)
                    dve.tensor_tensor(y_low[:, y:y + 2, :], pooled, y_high[:, y:y + 2, :].bitcast(F32),
                                      ALU.subtract).then_inc(pooled_lo, 1)

            def pool_slot(n, j):
                if j == 2 and n >= 2:
                    pool_result(n - 2)
                if j == 2 and n >= 1:
                    convert_aux(3 + n)
                if n >= 1:
                    pool_steps(n - 1, j)

            for n in range(4):
                for j in range(PAIR_UNITS):
                    convert(8 + n, j)
                    if n < 2:
                        heads_tail(3, PAIR_UNITS * n + j)
                    pool_slot(n, j)

            def add_pair(buf, p):
                r = resid[:, bass.ds(2 * p, 2), :].rearrange("p k (a t) -> p k a t", a=2)
                dve.tensor_tensor(r, ps[:, 4 * buf:4 * buf + 4, 0:HALF].rearrange("p (k a) t -> p k a t", a=2), r,
                                  ALU.add).then_inc(pair_evac, 1)

            def out_steps(o, buf):
                dve.wait_ge(unit_used, 8 * o + 104)
                add_pair(buf, o)
                for t in range(2):
                    c = 2 * o + t
                    dve.wait_ge(h2_hi, c + 1)
                    dve.scalar_tensor_tensor(out=h_low[:, bass.ds(c, 1), :].rearrange("p k t -> p (k t)"),
                                             in0=resid[:, bass.ds(c, 1), :].rearrange("p k t -> p (k t)"),
                                             scalar=column("g_mlp", c),
                                             in1=h_high[:, bass.ds(c, 1), :].rearrange("p k t -> p (k t)").bitcast(F32),
                                             op0=ALU.mult, op1=ALU.subtract).then_inc(h2_lo, 1)
                dve.wait_ge(out_sq, o + 1)
                if isinstance(o, int) and o == 0:
                    dve.memset(sel[:, 0:1], 0.0).then_inc(sq_summed, 1)
                else:
                    dve.wait_ge(sq_summed, o)
                    dve.tensor_tensor(scratch[:, 2:4, :], scratch[:, 2:4, :], scratch[:, 0:2, :], ALU.add).then_inc(sq_summed, 1)

            for n in range(2):
                for j in range(PAIR_UNITS):
                    convert(IN_PAIRS + n, j)
                    if n == 0:
                        pool_slot(4, j)
                        if j == 6:
                            dve.wait_ge(pooled_lo, 4)
                            settle()
                            dve.memset(sel[:, 0:1], 0.0).then_inc(last_ready, 1)
                        if j == 7:
                            pool_result(3)
                    elif j == 2:
                        dve.wait_ge(last_t, 4)
                        for m, rows in enumerate((72, 88, 120, 64)):
                            dve.tensor_copy(aux_raw[0:rows, m * P:(m + 1) * P], ps[0:rows, 4 + m, 0:P]).then_inc(last_copied, 1)
                        step(dve.tensor_copy(resid[:, :, PROMPT:TOK], xs_t[:].rearrange("p (b c) -> p c b", b=SAMPLES)))
                        dve.wait_ge(x_back, 64)
                        settle()
                    elif j == 4:
                        out_steps(0, 0)
            with dve.Fori(1, OUT_PAIRS // 2) as b:
                for half in range(2):
                    for j in range(PAIR_UNITS):
                        convert(2 * b + (IN_PAIRS + half), j)
                        if j == 4:
                            out_steps(2 * b + (half - 1), 1 - half)

            def up_steps(m, buf):
                ends = m // 8 if isinstance(m, int) else None
                for t in range(2):
                    dve.scalar_tensor_tensor(out=halves(scratch[:, t, :]), in0=bank(buf, t), scalar=0.0, in1=halves(rstd[:]),
                                             op0=ALU.max, op1=ALU.mult).then_inc(f_relu, 1)

            def up_low(m, p):
                dve.wait_ge(f_relu, 2 * m + 2)
                dve.wait_ge(f_hi, m + 1)
                dve.memset(sel[:, 0:1], 0.0).then_inc(pair_evac, 1)
                dve.tensor_tensor(y_low[:, bass.ds(2 * p, 2), :], scratch[:, 0:2, :],
                                  y_high[:, bass.ds(2 * p, 2), :].bitcast(F32), ALU.subtract).then_inc(f_lo, 1)

            def up(g, p, buf):
                dve.wait_ge(unit_used, 128 * g + 8 * p + 168)
                up_steps(8 * g + p, buf)
                up_low(8 * g + p, p)

            def down(g, p, buf):
                dve.wait_ge(unit_used, 128 * g + 8 * p + 232)
                add_pair(buf, p)

            def final(p):
                if p == 0:
                    dve.wait_ge(out_sq, OUT_PAIRS + 1)
                    dve.memset(sel[:, 0:1], 0.0).then_inc(final_sq, 1)
                else:
                    dve.wait_ge(out_sq, OUT_PAIRS + 1 + p)
                    dve.wait_ge(final_sq, p)
                    dve.tensor_tensor(scratch[:, 2:4, :], scratch[:, 2:4, :], scratch[:, 0:2, :], ALU.add).then_inc(final_sq, 1)

            def quarter(g, before, last):
                for j in range(PAIR_UNITS):
                    convert(16 * g + 20, j)
                    if j == 3:
                        before()
                for j in range(PAIR_UNITS):
                    convert(16 * g + 21, j)
                    if j == 4:
                        up(g, 0, 0)
                with dve.Fori(1, MLP_PAIRS // 2) as b:
                    for half in range(2):
                        for j in range(PAIR_UNITS):
                            convert(16 * g + 2 * b + (20 + half), j)
                            if j == 4:
                                up(g, 2 * b + (half - 1), 1 - half)
                for j in range(PAIR_UNITS):
                    convert(16 * g + 28, j)
                    if j == 3:
                        up(g, 7, 1)
                for j in range(PAIR_UNITS):
                    convert(16 * g + 29, j)
                    if j == 4:
                        down(g, 0, 0)
                        if last:
                            final(0)
                if not last:
                    with dve.Fori(1, MLP_PAIRS // 2) as b:
                        for half in range(2):
                            for j in range(PAIR_UNITS):
                                convert(16 * g + 2 * b + (28 + half), j)
                                if j == 4:
                                    down(g, 2 * b + (half - 1), 1 - half)
                else:
                    for p in range(2, MLP_PAIRS):
                        for j in range(PAIR_UNITS):
                            convert(16 * g + p + 28, j)
                            if j == 4:
                                down(g, p - 1, (p - 1) % 2)
                                final(p - 1)

            def after_out():
                out_steps(OUT_PAIRS - 1, 1)
                dve.wait_ge(total_ready, 2)
                dve.tensor_scalar(halves(scratch[:, 0, :]), ps[:, 4:6, 0:HALF], 1.0 / D, EPS, ALU.mult,
                                  ALU.add).then_inc(mean_ready, 1)
                dve.wait_ge(root_ready, 2)
                dve.wait_ge(mean_ready, 2)
                step(newton(rstd[:], scratch[:, 0, :], scratch[:, 1, :], scratch[:, 1, :]))
                settle()

            quarter(0, after_out, False)
            with dve.Fori(1, GROUPS - 1) as g:
                quarter(g, lambda: down(g - 1, 7, 1), False)
            quarter(GROUPS - 1, lambda: down(GROUPS - 2, 7, 1), True)
            down(GROUPS - 1, 7, 1)
            final(7)
            dve.wait_ge(final_total, 1)
            for rows, a, b in ((P, 0, 4), (SAMPLES, 4, 5)):
                step(dve.tensor_scalar(r_final[0:rows, 0, a:b], ps[0:rows, 0, a:b], 1.0 / D, EPS, ALU.mult, ALU.add))
            settle()
            dve.memset(sel[:, 0:1], 0.0).then_inc(final_rstd, 1)
            dve.wait_ge(root_ready, 3)
            newton(r_final[:, 3, :], r_final[:, 0, :], r_final[:, 2, :], r_final[:, 1, :]).then_inc(final_rstd, 1)
            dve.wait_ge(final_rstd, 2)
            for m in range(1, 20, 2):
                t, rows = m // 4, P if m < 16 else SAMPLES
                dve.wait_ge(y_t, m + 1)
                if m >= RING:
                    dve.wait_ge(y_stored[m % RING], 16 * (m // RING))
                dve.tensor_scalar(raw[0:rows, m % RING, :], ps[0:rows, 1 + m % 7, :], r_final[0:rows, 3, t:t + 1], None,
                                  ALU.mult).then_inc(y_odd, 1)


_INS = ["x_prompt", "x_sample", "state_lru_h", "state_conv", "state_pool", "norm_mix_g", "w_in", "conv_w", "conv_b",
        "w_rg_a", "b_rg_a", "w_rg_x", "b_rg_x", "lru_lambda", "w_pool", "pool_scale", "w_out", "norm_mlp_g", "w_up",
        "w_down", "norm_final_g"]
_OUTS = [(1, 512, 2048), (8, 1, 2048), (1, 1, 1024), (1, 1, 3, 1024), (1, 1, 15, 1024), (1, 8, 1024), (1, 8, 3, 1024),
         (1, 8, 15, 1024)]


def kernel(**inputs):
    import numpy as _np
    import concourse.bacc as _bacc
    from concourse import mybir as _mybir
    from concourse.bass_utils import run_bass_kernel_spmd as _run

    nc = _bacc.Bacc("TRN2", target_bir_lowering=False, num_devices=1)
    arrays, args = {}, []
    for name in _INS:
        a = _np.ascontiguousarray(inputs[name])
        arrays[f"in_{name}_dram"] = a
        args.append(nc.dram_tensor(f"in_{name}_dram", a.shape, _mybir.dt.from_np(a.dtype), kind="ExternalInput").ap())
    for i, shape in enumerate(_OUTS):
        args.append(nc.dram_tensor(f"out_{i}_dram", shape, _mybir.dt.float32, kind="ExternalOutput").ap())
    build(nc, *args)
    r = _run(nc, [arrays], core_ids=[0])
    return tuple(r.results[0][f"out_{i}_dram"] for i in range(len(_OUTS)))
```

```python
from contextlib import ExitStack

import concourse.bass as bass
from concourse import mybir

F32 = mybir.dt.float32
F32R = mybir.dt.float32r
ALU = mybir.AluOpType
ACT = mybir.ActivationFunctionType
AX_X = mybir.AxisListType.X

P = 128
D = 2048
KC = D // P
PROMPT = 512
SAMPLES = 8
TOK = PROMPT + SAMPLES
HALF = TOK // 2
W_LRU = 1024
HEADS = W_LRU // P
CONV_W = 4
WINDOWS = (2, 4, 8, 16)
POOL_BUF = 15
GROUPS = 4
EPS = 1e-6
UNIT = 2 * 256
RING = 4
PAIR_UNITS = 8
IN_PAIRS, OUT_PAIRS, MLP_PAIRS = 12, 8, 8
SQRT_2_OVER_PI = 0.7978845608028654
GELU_CUBIC = 0.044715

EXT = 3 + TOK + CONV_W * SAMPLES + 1
EXT_S = 3 + TOK
CONV = EXT_S + CONV_W * (SAMPLES - 1) + 1
PEXT = POOL_BUF + TOK + (POOL_BUF + 1) * SAMPLES
PEXT_S = POOL_BUF + TOK

ROWS_OF = {}
_at = 0
for _name, _n in (("g_mix", KC), ("g_mlp", KC), ("g_final", KC), ("conv_w", CONV_W * HEADS), ("conv_b", HEADS),
                  ("b_a", HEADS), ("b_x", HEADS), ("lam", HEADS), ("pool_scale", HEADS)):
    ROWS_OF[_name] = _at
    _at += _n
VECTORS = _at

ST_LRU, ST_CONV = 0, SAMPLES * HEADS
ST_POOL = ST_CONV + SAMPLES * 3 * HEADS
ST_COLS = ST_POOL + SAMPLES * POOL_BUF * HEADS


class Order:

    def __init__(self, eng, sem):
        self.eng, self.sem, self.count, self.shift = eng, sem, 0, 0

    def mark(self, ins):
        ins.then_inc(self.sem, 1)
        self.count += 1

    def settle(self):
        self.eng.wait_ge(self.sem, self.shift + self.count)

    def enter(self, turn, per_turn):
        self.saved, self.base, self.per_turn = self.shift, self.count, per_turn
        self.shift = self.shift + turn * per_turn

    def leave(self, turns):
        assert self.count - self.base == self.per_turn, (self.count - self.base, self.per_turn)
        self.shift, self.count = self.saved, self.base + turns * self.per_turn


def build(nc, x_prompt, x_sample, state_lru_h, state_conv, state_pool, norm_mix_g, w_in, conv_w, conv_b,
          w_rg_a, b_rg_a, w_rg_x, b_rg_x, lru_lambda, w_pool, pool_scale, w_out, norm_mlp_g, w_up, w_down,
          norm_final_g, y_prompt, y_sample, lru_prompt, conv_prompt, pool_prompt, lru_sample, conv_sample,
          pool_sample):
    with ExitStack() as ctx:
        def sb(name, shape, dt=F32):
            return ctx.enter_context(nc.sbuf_tensor(name, shape, dt))

        def sem(name):
            return ctx.enter_context(nc.semaphore(name))

        h_high = sb("h_high", [P, KC, TOK], F32R)
        h_low = sb("h_low", [P, KC, TOK], F32R)
        y_high = sb("y_high", [P, KC, TOK], F32R)
        y_low = sb("y_low", [P, KC, TOK], F32R)
        resid = sb("resid", [P, KC, TOK])
        raw = sb("raw", [P, RING, UNIT])
        w_high = sb("w_high", [P, RING, 2, 256], F32R)
        w_low = sb("w_low", [P, RING, 2, 256], F32R)
        aux_raw = sb("aux_raw", [P, UNIT])
        aux_high = sb("aux_high", [P, UNIT], F32R)
        aux_low = sb("aux_low", [P, UNIT], F32R)
        rstd = sb("rstd", [P, TOK])
        scratch = sb("scratch", [P, 4, TOK])
        ident = sb("ident", [P, P])
        ones = sb("ones", [P, P])
        vec = sb("vec", [P, P])
        half_bias = sb("half_bias", [P, 2 * HEADS])
        lru_c = sb("lru_c", [P, 2, HEADS])
        tiny = sb("tiny", [P, 4, HEADS])
        xs_t = sb("xs_t", [P, P])
        xs_rows = sb("xs_rows", [P, P])
        inv_count = sb("inv_count", [P, POOL_BUF])
        sumsq = sb("sumsq", [P, 5])
        sq_parts = sb("sq_parts", [P, 4, 4])
        sel = sb("sel", [P, SAMPLES])
        lru_last = sb("lru_last", [P, 1 + SAMPLES, HEADS])
        conv_last = sb("conv_last", [P, 3 + SAMPLES, HEADS])
        pool_last = sb("pool_last", [P, POOL_BUF + SAMPLES, HEADS])
        r_final = sb("r_final", [P, 4, 5])
        ps = ctx.enter_context(nc.psum_tensor("ps", [P, 8, 512], F32))

        flat = resid[:].rearrange("p k t -> p (k t)")
        x_rows = flat[:, 0:4 * D].rearrange("p (t d) -> p t d", t=4)
        STATE_CHUNKS = 3 + SAMPLES
        state_rows = flat[:, 0:STATE_CHUNKS * P].rearrange("p (n f) -> p n f", n=STATE_CHUNKS)
        at = [0]

        def work(cols):
            at[0] += 2 * cols
            return flat[:, at[0] - 2 * cols:at[0]].rearrange("p (h t) -> p h t", h=2)

        conv_in = work(EXT)
        q = flat[:, 0:2 * TOK].rearrange("p (h t) -> p h t", h=2)
        conv_sum = work(CONV)
        gate = flat[:, 2 * EXT:2 * EXT + 2 * TOK].rearrange("p (h t) -> p h t", h=2)
        xc, tanh_x, tanh_a, decay = work(TOK), work(TOK), work(TOK), work(TOK)
        states = flat[:, at[0]:at[0] + ST_COLS]
        assert at[0] + ST_COLS <= KC * TOK
        at[0] = 0
        pool_in, sum_a, sum_b = work(PEXT), work(PEXT), work(PEXT)
        pooled, head_fix = work(TOK), work(POOL_BUF)
        y_rows = resid[:, :, 0:PROMPT]
        sample_squares = aux_raw[:].rearrange("p (a t) -> p a t", a=4)
        samples_y, samples_out = xs_rows, xs_t
        x_t_dram = nc.dram_tensor("x_t_spill", (KC, P, PROMPT), F32).ap()

        vectors_in, xs_in, states_in = sem("vectors_in"), sem("xs_in"), sem("states_in")
        x_in = [sem(f"x_in{b}") for b in range(4)]
        raw_in = [sem(f"raw_in{s}") for s in range(RING)]
        loads = sem("loads")
        aux_in, aux_hi, aux_lo = sem("aux_in"), sem("aux_hi"), sem("aux_lo")
        hi_ready, lo_ready, unit_used = sem("hi_ready"), sem("lo_ready"), sem("unit_used")
        ident_ready = sem("ident_ready")
        small_t, small_copied = sem("small_t"), sem("small_copied")
        x_t, x_hi, x_lo, x_staged = sem("x_t"), sem("x_hi"), sem("x_lo"), sem("x_staged")
        xs_scaled, xs_hi, xs_lo = sem("xs_scaled"), sem("xs_hi"), sem("xs_lo")
        spilled = [sem(f"spilled{s}") for s in range(4)]
        sumsq_ready, diag_ready, total_ready = sem("sumsq_ready"), sem("diag_ready"), sem("total_ready")
        mean_ready, root_ready = sem("mean_ready"), sem("root_ready")
        states_t, states_copied = sem("states_t"), sem("states_copied")
        lam_ready, lam_tanh = sem("lam_ready"), sem("lam_tanh")
        vec_order, act_order = sem("vector_order"), sem("scalar_order")
        ext_ready, tap0_ready, xc_ready = sem("ext_ready"), sem("tap0_ready"), sem("xc_ready")
        xc_hi, xc_lo, gates_mm = sem("xc_hi"), sem("xc_lo"), sem("gates_mm")
        gates_tanh, decay_exp, decay_tanh = sem("gates_tanh"), sem("decay_exp"), sem("decay_tanh")
        xi_ready, tanh_used, root_t = sem("xi_ready"), sem("tanh_used"), sem("root_t")
        gate_evac, gate_sq, gate_arg, gate_th = sem("gate_evac"), sem("gate_sq"), sem("gate_arg"), sem("gate_th")
        lru_y, y_hi, y_lo = sem("lru_y"), sem("y_hi"), sem("y_lo")
        pooled_ready, pooled_hi, pooled_lo, pool_mm = (sem("pooled_ready"), sem("pooled_hi"), sem("pooled_lo"),
                                                       sem("pool_mm"))
        last_ready, last_t, last_copied = sem("last_ready"), sem("last_t"), sem("last_copied")
        x_back = sem("x_back")
        pair_evac = sem("pair_evac")
        h2_hi, h2_lo, out_sq = sem("h2_hi"), sem("h2_lo"), sem("out_sq")
        sq_summed = sem("sq_summed")
        f_relu, f_sq, f_hi, f_lo = sem("f_relu"), sem("f_sq"), sem("f_hi"), sem("f_lo")
        final_sq, final_scaled, final_total = sem("final_sq"), sem("final_scaled"), sem("final_total")
        final_rstd, y_t, y_even, y_odd = sem("final_rstd"), sem("y_t"), sem("y_even"), sem("y_odd")
        y_stored, last_added, samples_sq, samples_ready = (sem("y_stored"), sem("last_added"), sem("samples_sq"),
                                                           sem("samples_ready"))
        states_stored = sem("states_stored")

        def bank(buf, tile):
            return ps[:, 4 * buf + 2 * tile:4 * buf + 2 * tile + 2, 0:HALF]

        def halves(v):
            return v.rearrange("p (a t) -> p a t", a=2)

        def column(name, c, step=None):
            return vec[:, bass.ds(ROWS_OF[name] + c, 1)]

        w_in_v = w_in[0].rearrange("(k p) e -> p k e", p=P)
        w_out_v = w_out[0].rearrange("(k p) e -> p k e", p=P)
        w_up_v = w_up[0].rearrange("(k p) e -> p k e", p=P)
        w_down_v = w_down[0].rearrange("(k p) e -> p k e", p=P)

        def pool_group(n):
            return len(WINDOWS) - 1 - n

        def y_row(slot):
            return slot if slot < HEADS else HEADS + 2 * pool_group((slot - HEADS) // 2) + slot % 2

        block = ctx.enter_context(nc.Block())

        @block.sync
        def _(sp):
            def load_x(b):
                sp.dma_start(x_rows[:, :, b * 512:(b + 1) * 512],
                             x_prompt[0, :, b * 512:(b + 1) * 512].rearrange("(t p) d -> p t d", p=P)).then_inc(x_in[b], 16)

            load_x(0)
            for name, src in (("g_mix", norm_mix_g[0]), ("g_mlp", norm_mlp_g[0]), ("g_final", norm_final_g),
                              ("conv_b", conv_b[0]), ("b_a", b_rg_a[0]), ("b_x", b_rg_x[0]),
                              ("lam", lru_lambda[0]), ("pool_scale", pool_scale[0])):
                rows = src.rearrange("(c f) -> c f", f=P)
                a = ROWS_OF[name]
                sp.dma_start(aux_raw[a:a + rows.shape[0], 0:P], rows).then_inc(vectors_in, 16)
            a = ROWS_OF["conv_w"]
            sp.dma_start(aux_raw[a:a + CONV_W * HEADS, 0:P],
                         conv_w[0].rearrange("k (c f) -> (k c) f", f=P)).then_inc(vectors_in, 16)
            sp.dma_start(xs_rows[:], x_sample.rearrange("b s (c f) -> (b s c) f", f=P)).then_inc(xs_in, 16)

            def load(n, j, src, first=False):
                if not first:
                    sp.wait_ge(hi_ready, 8 * n + (j - 3))
                    sp.wait_ge(lo_ready, 8 * n + (j - 3))
                    sp.sem_inc(loads, 1)
                sp.dma_start(raw[:, j % RING, :].rearrange("p (k e) -> p k e", k=2), src).then_inc(raw_in[j % RING], 16)

            def load_heads(i):
                sp.dma_start(aux_raw[:, 0:256].rearrange("p (h e) -> p h e", h=2),
                             w_rg_a[0, bass.ds(2 * i, 2)].rearrange("h p e -> p h e")).then_inc(aux_in, 16)
                sp.dma_start(aux_raw[:, 256:512].rearrange("p (h e) -> p h e", h=2),
                             w_rg_x[0, bass.ds(2 * i, 2)].rearrange("h p e -> p h e")).then_inc(aux_in, 16)

            def load_x_unit(i, j, first=False):
                load(2 * i, j, w_in_v[:, 2 * j:2 * j + 2, bass.ds(256 * i, 256)], first)

            def heads_turn(i, first):
                for j in range(RING + 2 if first else 0, PAIR_UNITS):
                    load_x_unit(i, j)
                if first:
                    sp.wait_ge(small_t, 1)
                else:
                    sp.wait_ge(aux_hi, i)
                    sp.wait_ge(aux_lo, i)
                    sp.sem_inc(loads, 1)
                load_heads(i)
                for j in range(PAIR_UNITS):
                    load(2 * i + 1, j, w_in_v[:, 2 * j:2 * j + 2, bass.ds(W_LRU + 256 * i, 256)])

            for j in range(RING + 2):
                load_x_unit(0, j, j < RING)
                if j == 1:
                    load_x(1)
                elif j == 3:
                    sp.wait_ge(x_staged, 2)
                    load_x(2)
                elif j == 5:
                    sp.wait_ge(x_staged, 6)
                    load_x(3)
            heads_turn(0, True)
            with sp.Fori(1, 4) as i:
                heads_turn(i, False)
            with sp.Fori(0, 4) as n:
                for j in range(PAIR_UNITS):
                    load(8 + n, j, w_in_v[:, 2 * j:2 * j + 2, bass.ds(2 * W_LRU + 768 - 256 * n, 256)])
                sp.wait_ge(aux_hi, 4 + n)
                sp.wait_ge(aux_lo, 4 + n)
                sp.sem_inc(loads, 1)
                sp.dma_start(aux_raw[:].rearrange("p (k e) -> p k e", k=2),
                             w_pool[0, bass.ds(3 - n, 1)].rearrange("g (k p) e -> p (g k) e", p=P)).then_inc(aux_in, 16)
            with sp.Fori(0, OUT_PAIRS) as o:
                for j in range(PAIR_UNITS):
                    load(IN_PAIRS + o, j, w_out_v[:, y_row(2 * j):y_row(2 * j) + 2, bass.ds(256 * o, 256)])
            with sp.Fori(0, GROUPS) as g:
                with sp.Fori(0, MLP_PAIRS) as p:
                    for j in range(PAIR_UNITS):
                        load(20 + 16 * g + p, j, w_up_v[:, 2 * j:2 * j + 2, bass.ds(2048 * g + 256 * p, 256)])
                with sp.Fori(0, MLP_PAIRS) as p:
                    for j in range(PAIR_UNITS):
                        load(28 + 16 * g + p, j, w_down_v[:, bass.ds(16 * g + 2 * j, 2), bass.ds(256 * p, 256)])

            for m in range(16):
                c, t = m // 4, m % 4
                sp.wait_ge(y_even if m % 2 == 0 else y_odd, m // 2 + 1)
                sp.dma_start(y_prompt[0, t * P:(t + 1) * P, c * 512:(c + 1) * 512], y_rows[:, m, :]).then_inc(y_stored, 16)
            sp.wait_ge(y_even, 9)
            sp.dma_start(y_sample.rearrange("b s (c f) -> (b s c) f", f=P), samples_out[:]).then_inc(y_stored, 16)
            sp.wait_ge(y_stored, 16 * 17)

        @block.gpsimd
        def _(pool):
            pool.memset(ident[:], 0.0).then_inc(ident_ready, 1)
            pool.wait_ge(ident_ready, 1)
            pool.affine_select(out=ident[:], in_=ident[:], compare_op=ALU.not_equal, fill=1.0, base=0,
                               pattern=[[-1, P]], channel_multiplier=1).then_inc(ident_ready, 1)
            pool.dma_start(conv_sample[0, :, 0:2, :], state_conv[0, :, 1:3, :]).then_inc(states_stored, 16)
            pool.dma_start(pool_sample[0, :, 0:POOL_BUF - 1, :], state_pool[0, :, 1:POOL_BUF, :]).then_inc(states_stored, 16)
            for k in range(KC):
                pool.wait_ge(x_staged, k + 1)
                pool.dma_start(x_t_dram[k], scratch[:, k % 4, 0:PROMPT]).then_inc(spilled[k % 4], 16)
                if k == STATE_CHUNKS + 1:
                    pool.wait_ge(x_t, STATE_CHUNKS)
                    pool.wait_ge(sumsq_ready, 1 + 4 * ((STATE_CHUNKS - 1) // 4) + 1)
                    pool.dma_start(state_rows[0:64, 0, :],
                                   state_lru_h[0].rearrange("b (c f) -> (b c) f", f=P)).then_inc(states_in, 16)
                    pool.dma_start(state_rows[0:96, 1:3, :],
                                   state_conv[0].rearrange("(t b) k (c f) -> (b k c) t f", t=2, f=P)).then_inc(states_in, 16)
                    pool.dma_start(state_rows[0:120, 3:11, :],
                                   state_pool[0].rearrange("b k (c f) -> (k c) b f", f=P)).then_inc(states_in, 16)
            pool.wait_ge(pooled_lo, 4)
            pool.wait_ge(pooled_hi, 4)
            pool.wait_ge(last_ready, 1)
            for s in spilled:
                pool.wait_ge(s, 16 * 4)
            for c in range(4):
                pool.dma_start(resid[:, 4 * c:4 * c + 4, 0:PROMPT],
                               x_t_dram[4 * c:4 * c + 4].rearrange("k p t -> p k t")).then_inc(x_back, 16)
            pool.wait_ge(last_copied, 4)
            rows = aux_raw[:].rearrange("p (n f) -> p n f", n=4)
            pool.dma_start(lru_prompt[0, 0, :].rearrange("(c f) -> c f", f=P), rows[0:8, 0, :]).then_inc(states_stored, 16)
            pool.dma_start(lru_sample[0].rearrange("b (c f) -> (b c) f", f=P), rows[8:72, 0, :]).then_inc(states_stored, 16)
            pool.dma_start(conv_prompt[0, 0].rearrange("k (c f) -> (k c) f", f=P), rows[0:24, 1, :]).then_inc(states_stored, 16)
            for b in range(SAMPLES):
                pool.dma_start(conv_sample[0, b, 2, :].rearrange("(c f) -> c f", f=P),
                               rows[24 + 8 * b:32 + 8 * b, 1, :]).then_inc(states_stored, 16)
            pool.dma_start(pool_prompt[0, 0].rearrange("k (c f) -> (k c) f", f=P), rows[0:120, 2, :]).then_inc(states_stored, 16)
            for b in range(SAMPLES):
                pool.dma_start(pool_sample[0, b, POOL_BUF - 1, :].rearrange("(c f) -> c f", f=P),
                               rows[8 * b:8 * b + 8, 3, :]).then_inc(states_stored, 16)
            pool.wait_ge(states_stored, 16 * (6 + 2 * SAMPLES))

        @block.tensor
        def _(pe):
            def unit(n, j, buf, high, low):
                pe.wait_ge(hi_ready, 8 * n + (j + 1))
                pe.wait_ge(lo_ready, 8 * n + (j + 1))
                s = j % RING
                for kk in range(2):
                    k = 2 * j + kk
                    first, last = k == 0, k == KC - 1
                    for t in range(2):
                        wh, wl = (w[:, s, kk, t * P:(t + 1) * P] for w in (w_high, w_low))
                        for a in range(2):
                            out = ps[:, 4 * buf + 2 * t + a, 0:HALF]
                            pe.matmul(out, wh, high[:, k, a * HALF:(a + 1) * HALF], start=first, stop=False)
                        for a in range(2):
                            out = ps[:, 4 * buf + 2 * t + a, 0:HALF]
                            pe.matmul(out, wh, low[:, k, a * HALF:(a + 1) * HALF], start=False, stop=False)
                        for a in range(2):
                            out = ps[:, 4 * buf + 2 * t + a, 0:HALF]
                            mm = pe.matmul(out, wl, high[:, k, a * HALF:(a + 1) * HALF], start=False, stop=last)
                mm.then_inc(unit_used, 1)

            def split_product(banks, w_col, terms, done):
                for a in range(2):
                    out = ps[:, banks + a, 0:HALF]
                    for m, (slot, col) in enumerate(terms):
                        wh, wl = aux_high[:, col:col + P], aux_low[:, col:col + P]
                        xh = y_high[:, bass.ds(slot, 1), a * HALF:(a + 1) * HALF]
                        xl = y_low[:, bass.ds(slot, 1), a * HALF:(a + 1) * HALF]
                        pe.matmul(out, wh, xh, start=(m == 0), stop=False)
                        pe.matmul(out, wh, xl, start=False, stop=False)
                        mm = pe.matmul(out, wl, xh, start=False, stop=(m == len(terms) - 1))
                if done is not None:
                    mm.then_inc(done, 1)

            def gates(i, h):
                if h == 0:
                    pe.wait_ge(xc_hi, i + 1)
                    pe.wait_ge(xc_lo, i + 1)
                    pe.wait_ge(aux_hi, i + 1)
                    pe.wait_ge(aux_lo, i + 1)
                else:
                    pe.wait_ge(gates_tanh, 4 * i + 2)
                split_product(0, h * P, [(2 * i + h, h * P)], None)
                split_product(2, (2 + h) * P, [(2 * i + h, (2 + h) * P)], gates_mm)

            def pool_product(n):
                pe.wait_ge(pooled_hi, n + 1)
                pe.wait_ge(pooled_lo, n + 1)
                pe.wait_ge(aux_hi, 5 + n)
                pe.wait_ge(aux_lo, 5 + n)
                slots = (HEADS + 2 * n, HEADS + 2 * n + 1)
                for t in range(2):
                    split_product(4 * (n % 2) + 2 * t, None, [(slots[k], k * 256 + t * P) for k in range(2)],
                                  pool_mm if t == 1 else None)

            def turn_x(k):
                if k % 4 == 0:
                    pe.wait_ge(x_in[k // 4], 16)
                if k >= 3:
                    pe.wait_ge(x_staged, k - 2)
                for t in range(4):
                    mm = pe.transpose(ps[:, 4 + k % 3, t * P:(t + 1) * P], x_rows[:, t, k * P:(k + 1) * P], ident[:])
                mm.then_inc(x_t, 1)

            pe.wait_ge(ident_ready, 2)
            for k in range(3):
                turn_x(k)
            pe.wait_ge(vectors_in, 16 * 9)
            pe.transpose(ps[:, 3, 0:VECTORS], aux_raw[0:VECTORS, 0:P], ident[0:VECTORS, 0:VECTORS]).then_inc(small_t, 1)
            pe.wait_ge(xs_in, 16)
            pe.transpose(ps[:, 3, P:2 * P], xs_rows[:], ident[:]).then_inc(small_t, 1)
            turn_x(3)

            pe.wait_ge(small_copied, 2)
            pe.wait_ge(xs_hi, 1)
            pe.wait_ge(xs_lo, 1)
            for j in range(PAIR_UNITS):
                if 1 <= j < PAIR_UNITS - 1:
                    turn_x(2 * j + 2)
                    turn_x(2 * j + 3)
                if j == PAIR_UNITS - 1:
                    pe.wait_ge(x_staged, KC)
                    pe.wait_ge(vec_order, 1)
                    pe.wait_ge(diag_ready, 5)
                    pe.matmul(ps[:, 7, 0:256], ones[:], rstd[:, 0:256], start=True, stop=True)
                    pe.matmul(ps[:, 7, 256:512], ones[:], rstd[:, 256:512], start=True, stop=True)
                    pe.matmul(ps[:, 4, 504:512], ones[:], rstd[:, 512:520], start=True, stop=True).then_inc(total_ready, 1)
                    pe.wait_ge(states_in, 48)
                    pe.transpose(ps[:, 4, 0:64], state_rows[0:64, 0, :], ident[0:64, 0:64])
                    for t in range(2):
                        pe.transpose(ps[:, 4, 64 + 96 * t:160 + 96 * t], state_rows[0:96, 1 + t, :], ident[0:96, 0:96])
                    for b in range(SAMPLES):
                        mm = pe.transpose(ps[:, 5 + b // 4, 120 * (b % 4):120 * (b % 4) + 120], state_rows[0:120, 3 + b, :],
                                          ident[0:120, 0:120])
                    mm.then_inc(states_t, 1)
                pe.wait_ge(x_hi, 2 * j + 2)
                pe.wait_ge(x_lo, 2 * j + 2)
                unit(0, j, 0, h_high, h_low)

            def gate_pair(i, first):
                if first:
                    pe.wait_ge(states_copied, 2)
                    pe.wait_ge(mean_ready, 1)
                else:
                    pe.wait_ge(gate_evac, 2 * i)
                for j in range(PAIR_UNITS):
                    unit(2 * i + 1, j, 1, h_high, h_low)
                    if j == 5:
                        gates(i, 0)
                    if j == 6:
                        gates(i, 1)

            gate_pair(0, True)
            with pe.Fori(1, 4) as i:
                pe.wait_ge(gates_tanh, 4 * i)
                for j in range(PAIR_UNITS):
                    unit(2 * i, j, 0, h_high, h_low)
                gate_pair(i, False)

            for n in range(4):
                if n == 0:
                    pe.wait_ge(gates_tanh, 16)
                elif n == 1:
                    pe.wait_ge(gate_evac, 8)
                else:
                    pe.wait_ge(pair_evac, n - 1)
                for j in range(PAIR_UNITS):
                    unit(8 + n, j, n % 2, h_high, h_low)
                    if n >= 1 and j == 6:
                        pool_product(n - 1)

            def out_unit(o, j, buf):
                unit(IN_PAIRS + o, j, buf, y_high, y_low)

            pe.wait_ge(pair_evac, 3)
            pe.wait_ge(y_hi, 4)
            pe.wait_ge(y_lo, 4)
            for j in range(PAIR_UNITS):
                if j >= 4:
                    pe.wait_ge(y_hi, 4 + 2 * (j - 3))
                    pe.wait_ge(y_lo, 4 + 2 * (j - 3))
                out_unit(0, j, 0)
                if j == 3:
                    pool_product(3)
            pe.wait_ge(pair_evac, 4)
            pe.wait_ge(last_ready, 1)
            for m, (rows, last) in enumerate(((72, lru_last[:]), (88, conv_last[:]), (120, pool_last[:, 0:POOL_BUF, :]),
                                              (64, pool_last[:, POOL_BUF:POOL_BUF + SAMPLES, :]))):
                pe.transpose(ps[0:rows, 4 + m, 0:P], last.rearrange("p j c -> p (j c)"), ident[:]).then_inc(last_t, 1)
            pe.wait_ge(last_copied, 4)
            for j in range(PAIR_UNITS):
                out_unit(1, j, 1)
            with pe.Fori(1, OUT_PAIRS // 2) as b:
                for half in range(2):
                    pe.wait_ge(pair_evac, 2 * b + (half + 3))
                    for j in range(PAIR_UNITS):
                        out_unit(2 * b + half, j, half)

            def up_unit(g, b, half, j):
                unit(16 * g + 2 * b + (20 + half), j, half, h_high, h_low)

            def up_pairs(g, start):
                with pe.Fori(start, MLP_PAIRS // 2) as b:
                    for half in range(2):
                        pe.wait_ge(pair_evac, 16 * g + 2 * b + (half + 11))
                        for j in range(PAIR_UNITS):
                            up_unit(g, b, half, j)

            def down_pairs(g):
                with pe.Fori(0, MLP_PAIRS // 2) as b:
                    for half in range(2):
                        pe.wait_ge(pair_evac, 16 * g + 2 * b + (half + 19))
                        for j in range(PAIR_UNITS):
                            if half == 0:
                                pe.wait_ge(f_hi, 8 * g + (j + 1))
                                pe.wait_ge(f_lo, 8 * g + (j + 1))
                            unit(16 * g + 2 * b + (28 + half), j, half, y_high, y_low)

            pe.wait_ge(pair_evac, 11)
            for j in range(PAIR_UNITS):
                pe.wait_ge(h2_hi, 2 * j + 2)
                pe.wait_ge(h2_lo, 2 * j + 2)
                up_unit(0, 0, 0, j)
                if j == 4:
                    pe.wait_ge(sq_summed, OUT_PAIRS)
                    pe.wait_ge(pair_evac, 12)
                    for a in range(2):
                        for t in range(2):
                            mm = pe.matmul(ps[:, 4 + a, 0:HALF], ones[:], scratch[:, 2 + t, a * HALF:(a + 1) * HALF],
                                           start=(t == 0), stop=(t == 1))
                    mm.then_inc(total_ready, 1)
            pe.wait_ge(mean_ready, 2)
            for j in range(PAIR_UNITS):
                up_unit(0, 0, 1, j)
            up_pairs(0, 1)
            down_pairs(0)
            with pe.Fori(1, GROUPS) as g:
                up_pairs(g, 0)
                down_pairs(g)

            def totals(col, tiles):
                for t in range(4):
                    for a in range(2):
                        mm = pe.matmul(ps[:, 0, col + t:col + t + 1], scratch[:, tiles + a, t * P:(t + 1) * P], ones[:, 0:1],
                                       start=(a == 0), stop=(a == 1))
                return mm

            def turn_back(m):
                c, t = m // 4, m % 4
                if t == 0:
                    pe.wait_ge(final_scaled, 2 * c + (3 if c == 3 else 2))
                if m >= 7:
                    pe.wait_ge(y_even if (m - 7) % 2 == 0 else y_odd, (m - 7) // 2 + 1)
                for f in range(4):
                    mm = pe.transpose(ps[:, 1 + m % 7, f * P:(f + 1) * P], resid[:, 4 * c + f, t * P:(t + 1) * P],
                                      ident[:])
                mm.then_inc(y_t, 1)

            pe.wait_ge(pair_evac, 75)
            pe.wait_ge(final_sq, OUT_PAIRS - 1)
            totals(0, 2)
            for m in range(3):
                turn_back(m)
            pe.wait_ge(out_sq, 2 * OUT_PAIRS + 1)
            totals(4, 0)
            pe.wait_ge(samples_sq, 3)
            pe.matmul(ps[:, 0, 8:9], sample_squares[:, 0, :], ones[:, 0:1], start=True, stop=True).then_inc(final_total, 1)
            pe.wait_ge(pair_evac, 76)
            for m in range(3, 16):
                turn_back(m)
            pe.wait_ge(samples_ready, 1)
            pe.wait_ge(final_rstd, 1)
            pe.transpose(ps[:, 0, P:2 * P], samples_y[:], ident[:]).then_inc(y_t, 1)

        @block.scalar
        def _(act):
            order = Order(act, act_order)

            def convert(n, j, first=False):
                act.wait_ge(raw_in[j % RING], 32 * n + 16 * (j // RING + 1))
                if not first:
                    act.wait_ge(unit_used, 8 * n + (j - 3))
                act.activation(w_high[:, j % RING].rearrange("p k e -> p (k e)"), raw[:, j % RING, :],
                               ACT.Copy).then_inc(hi_ready, 1)

            def convert_aux(m, landed, user, used):
                act.wait_ge(aux_in, landed)
                if user is not None:
                    act.wait_ge(user, used)
                act.activation(aux_high[:], aux_raw[:], ACT.Copy).then_inc(aux_hi, 1)

            def root(m):
                act.wait_ge(mean_ready, m)
                act.activation(scratch[:, 1, :], scratch[:, 0, :], ACT.Sqrt).then_inc(root_ready, 1)

            def squares(j):
                b = j // 2
                act.wait_ge(x_in[b], 16)
                for t in (2 * (j % 2), 2 * (j % 2) + 1):
                    act.wait_ge(sumsq_ready, 4 * b + t + 1)
                    act.activation(ps[:, 7, :], x_rows[:, t, b * 512:(b + 1) * 512], ACT.Square,
                                   accum_out=sq_parts[:, t, b:b + 1]).then_inc(sumsq_ready, 1)

            def heads_tail(i, j):
                if j == 2:
                    gate_activations(i, 1)
                if j == 4:
                    act.wait_ge(tanh_used, i + 1)
                    act.activation(tanh_a, tanh_a, ACT.Sqrt).then_inc(root_t, 1)
                    act.wait_ge(gate_evac, 2 * i + 2)
                    act.wait_ge(xi_ready, i + 1)
                    act.activation(tanh_x, gate, ACT.Square).then_inc(gate_sq, 1)
                if j == 8:
                    act.wait_ge(gate_arg, i + 1)
                    act.activation(tanh_x, tanh_x, ACT.Tanh, scale=SQRT_2_OVER_PI).then_inc(gate_th, 1)
                if j == 9:
                    act.wait_ge(lru_y, i + 1)
                    act.activation(y_high[:, bass.ds(2 * i, 2), :], gate, ACT.Copy).then_inc(y_hi, 1)

            def gate_activations(i, h):
                act.wait_ge(gates_mm, 2 * i + (h + 1))
                act.activation(halves(tanh_a[:, h]), bank(0, 0), ACT.Tanh, scale=0.5,
                               bias=half_bias[:, bass.ds(2 * i + h, 1)]).then_inc(gates_tanh, 1)
                act.activation(halves(tanh_x[:, h]), bank(0, 1), ACT.Tanh, scale=0.5,
                               bias=half_bias[:, bass.ds(2 * i + h + HEADS, 1)]).then_inc(gates_tanh, 1)
                act.wait_ge(gates_tanh, 4 * i + (2 * h + 1))
                act.activation(q[:, h], tanh_a[:, h], ACT.Exp, scale=lru_c[:, 1, bass.ds(2 * i + h, 1)],
                               bias=lru_c[:, 1, bass.ds(2 * i + h, 1)]).then_inc(decay_exp, 1)
                act.activation(tanh_a[:, h], tanh_a[:, h], ACT.Tanh, scale=lru_c[:, 0, bass.ds(2 * i + h, 1)],
                               bias=lru_c[:, 0, bass.ds(2 * i + h, 1)]).then_inc(decay_tanh, 1)

            def gate_slot(i, j):
                if j == 0:
                    convert_aux(i, 32 * i + 32, None if isinstance(i, int) else gates_mm, 2 * i)
                if j == 4:
                    for h in range(2):
                        if h == 0:
                            act.wait_ge(ext_ready, i + 1)
                        act.activation(conv_sum[:, h], conv_in[:, h, 0:CONV], ACT.Identity,
                                       scale=column("conv_w", 2 * i + h),
                                       bias=column("conv_b", 2 * i + h)).then_inc(tap0_ready, 1)
                if j == 6:
                    act.wait_ge(xc_ready, i + 1)
                    act.activation(y_high[:, bass.ds(2 * i, 2), :], xc, ACT.Copy).then_inc(xc_hi, 1)
                if j == 7:
                    gate_activations(i, 0)

            for j in range(PAIR_UNITS):
                convert(0, j, j < RING)
                if j > 0:
                    squares(j)
                if j == 0:
                    act.wait_ge(small_copied, 1)
                for k in (2 * j, 2 * j + 1):
                    act.wait_ge(x_staged, k + 1)
                    act.activation(h_high[:, k, 0:PROMPT], scratch[:, k % 4, 0:PROMPT], ACT.Copy,
                                   scale=column("g_mix", k)).then_inc(x_hi, 1)
                if j == 0:
                    act.wait_ge(xs_scaled, 1)
                    act.activation(h_high[:, :, PROMPT:TOK], rstd[:, 0:P].rearrange("p (c b) -> p c b", b=SAMPLES),
                                   ACT.Copy).then_inc(xs_hi, 1)
                    act.wait_ge(xs_in, 16)
                    act.wait_ge(lam_ready, 1)
                    act.activation(tiny[:, 1, :], tiny[:, 0, :], ACT.Tanh, scale=1.0 / 32.0).then_inc(lam_tanh, 1)
                    act.activation(ps[:, 7, 0:P], xs_rows[:], ACT.Square, accum_out=sumsq[:, 4:5]).then_inc(sumsq_ready, 1)
                if j == 0:
                    squares(j)
            for j in range(PAIR_UNITS):
                convert(1, j)
                if j == 2:
                    act.wait_ge(states_t, 1)
                    act.activation(states[:, ST_POOL:ST_COLS].rearrange("p (b t) -> p b t", b=2), ps[:, 5:7, 0:480],
                                   ACT.Copy).then_inc(states_copied, 1)
                    root(1)
                gate_slot(0, j)
            with act.Fori(1, 4) as i:
                for j in range(PAIR_UNITS):
                    convert(2 * i, j)
                    heads_tail(i - 1, j)
                for j in range(PAIR_UNITS):
                    convert(2 * i + 1, j)
                    heads_tail(i - 1, PAIR_UNITS + j)
                    gate_slot(i, j)

            def pool_result(n):
                act.wait_ge(pool_mm, n + 1)
                for t in range(2):
                    act.activation(halves(y_high[:, HEADS + 2 * n + t, :]), bank(n % 2, t), ACT.Copy,
                                   scale=column("pool_scale", 2 * pool_group(n) + t)).then_inc(y_hi, 1)

            def pool_slot(n, j):
                if j == 2 and n >= 2:
                    pool_result(n - 2)
                if j == 2 and n >= 1:
                    convert_aux(3 + n, 128 + 16 * n, pool_mm if n >= 2 else gates_mm, n - 1 if n >= 2 else 8)
                if j == 6 and n >= 1:
                    act.wait_ge(pooled_ready, n)
                    act.activation(y_high[:, HEADS + 2 * n - 2:HEADS + 2 * n, :], pooled, ACT.Copy).then_inc(pooled_hi, 1)

            for n in range(4):
                for j in range(PAIR_UNITS):
                    convert(8 + n, j)
                    if n < 2:
                        heads_tail(3, PAIR_UNITS * n + j)
                    pool_slot(n, j)

            def out_steps(o):
                act.wait_ge(pair_evac, o + 5)
                for t in range(2):
                    act.activation(h_high[:, bass.ds(2 * o + t, 1), :].rearrange("p k t -> p (k t)"),
                                   resid[:, bass.ds(2 * o + t, 1), :].rearrange("p k t -> p (k t)"), ACT.Copy,
                                   scale=column("g_mlp", 2 * o + t)).then_inc(h2_hi, 1)
                if isinstance(o, int) and o == 0:
                    act.wait_ge(spilled[2], 64)
                    act.wait_ge(spilled[3], 64)
                    act.activation(scratch[:, 2:4, :], resid[:, 0:2, :], ACT.Square).then_inc(out_sq, 1)
                else:
                    act.wait_ge(sq_summed, 1)
                    act.wait_ge(sq_summed, o)
                    act.activation(scratch[:, 0:2, :], resid[:, bass.ds(2 * o, 2), :], ACT.Square).then_inc(out_sq, 1)

            for n in range(2):
                for j in range(PAIR_UNITS):
                    convert(IN_PAIRS + n, j)
                    if n == 0:
                        pool_slot(4, j)
                        if j == 7:
                            pool_result(3)
                    elif j == 4:
                        out_steps(0)
            with act.Fori(1, OUT_PAIRS // 2) as b:
                for half in range(2):
                    for j in range(PAIR_UNITS):
                        convert(2 * b + (IN_PAIRS + half), j)
                        if j == 4:
                            out_steps(2 * b + (half - 1))

            def up_steps(m):
                act.wait_ge(f_relu, 2 * m + 2)
                act.activation(scratch[:, 0:2, :], scratch[:, 0:2, :], ACT.Square).then_inc(f_sq, 1)
                act.wait_ge(f_sq, m + 1)

            def up_high(m, p):
                act.activation(y_high[:, bass.ds(2 * p, 2), :], scratch[:, 0:2, :], ACT.Copy).then_inc(f_hi, 1)

            def final_steps(p):
                act.wait_ge(pair_evac, 69 + p)
                if p == 0:
                    act.activation(scratch[:, 2:4, :], resid[:, 0:2, :], ACT.Square).then_inc(out_sq, 1)
                    act.wait_ge(out_sq, OUT_PAIRS + 1)
                else:
                    act.wait_ge(final_sq, p)
                    act.activation(scratch[:, 0:2, :], resid[:, 2 * p:2 * p + 2, :], ACT.Square).then_inc(out_sq, 1)
                    act.wait_ge(out_sq, OUT_PAIRS + 1 + p)
                for t in range(2):
                    k = 2 * p + t
                    ins = act.activation(resid[:, k, :], resid[:, k, :], ACT.Copy, scale=column("g_final", k))
                ins.then_inc(final_scaled, 1)

            def final_last():
                k = KC - 2
                act.wait_ge(last_added, 1)
                act.wait_ge(final_sq, OUT_PAIRS - 1)
                act.activation(scratch[:, 0, :], resid[:, k, :], ACT.Square).then_inc(out_sq, 1)
                act.wait_ge(pair_evac, 76)
                act.activation(scratch[:, 1, :], resid[:, k + 1, :], ACT.Square).then_inc(out_sq, 1)
                act.wait_ge(samples_sq, 2)
                act.wait_ge(out_sq, 2 * OUT_PAIRS + 1)
                for t in range(2):
                    act.activation(resid[:, k + t, :], resid[:, k + t, :], ACT.Copy,
                                   scale=column("g_final", k + t)).then_inc(final_scaled, 1)

            def quarter(g, head, last):
                for j in range(PAIR_UNITS):
                    convert(16 * g + 20, j)
                    if j == 3 and head == "out":
                        out_steps(OUT_PAIRS - 1)
                for j in range(PAIR_UNITS):
                    convert(16 * g + 21, j)
                    if j == 0 and head == "out":
                        root(2)
                    if j == 4:
                        up_steps(8 * g)
                        up_high(8 * g, 0)
                with act.Fori(1, MLP_PAIRS // 2) as b:
                    for half in range(2):
                        for j in range(PAIR_UNITS):
                            convert(16 * g + 2 * b + (20 + half), j)
                            if j == 4:
                                up_steps(8 * g + 2 * b + (half - 1))
                                up_high(8 * g + 2 * b + (half - 1), 2 * b + (half - 1))
                for j in range(PAIR_UNITS):
                    convert(16 * g + 28, j)
                    if j == 3:
                        up_steps(8 * g + 7)
                        up_high(8 * g + 7, 7)
                if not last:
                    with act.Fori(1, MLP_PAIRS) as p:
                        for j in range(PAIR_UNITS):
                            convert(16 * g + p + 28, j)
                else:
                    for p in range(1, MLP_PAIRS):
                        for j in range(PAIR_UNITS):
                            convert(16 * g + p + 28, j)
                            if j == 4:
                                final_steps(p - 1)

            quarter(0, "out", False)
            with act.Fori(1, GROUPS - 1) as g:
                quarter(g, "down", False)
            quarter(GROUPS - 1, "down", True)
            final_last()
            act.wait_ge(final_rstd, 1)
            act.activation(r_final[:, 1, :], r_final[:, 0, :], ACT.Sqrt).then_inc(root_ready, 1)
            act.wait_ge(final_scaled, OUT_PAIRS + 1)
            act.activation(samples_y[:].rearrange("p (b c) -> p c b", b=SAMPLES), resid[:, :, PROMPT:TOK],
                           ACT.Copy).then_inc(samples_ready, 1)
            act.wait_ge(final_rstd, 2)
            for m in range(0, 16, 2):
                act.wait_ge(y_t, 4 * (m // 4) + 4)
                act.activation(y_rows[:, m, :], ps[:, 1 + m % 7, :], ACT.Copy,
                               scale=r_final[:, 3, m % 4:m % 4 + 1]).then_inc(y_even, 1)
            act.wait_ge(y_t, 17)
            act.activation(samples_out[:], ps[:, 0, P:2 * P], ACT.Copy, scale=r_final[:, 3, 4:5]).then_inc(y_even, 1)

        @block.vector
        def _(dve):
            order = Order(dve, vec_order)
            step = order.mark
            settle = order.settle

            def convert(n, j, first=False):
                dve.wait_ge(hi_ready, 8 * n + (j + 1))
                if not first:
                    dve.wait_ge(unit_used, 8 * n + (j - 3))
                s = j % RING
                dve.tensor_tensor(w_low[:, s].rearrange("p k e -> p (k e)"), raw[:, s, :],
                                  w_high[:, s].rearrange("p k e -> p (k e)").bitcast(F32),
                                  ALU.subtract).then_inc(lo_ready, 1)

            def convert_aux(m):
                dve.wait_ge(aux_hi, m + 1)
                dve.tensor_tensor(aux_low[:], aux_raw[:], aux_high[:].bitcast(F32), ALU.subtract).then_inc(aux_lo, 1)

            def newton(y, v, t, root):
                step(dve.reciprocal(y, root))
                settle()
                step(dve.tensor_tensor(t, y, y, ALU.mult))
                settle()
                step(dve.tensor_tensor(t, t, v, ALU.mult))
                settle()
                step(dve.tensor_scalar(t, t, -0.5, 1.5, ALU.mult, ALU.add))
                settle()
                return dve.tensor_tensor(y, y, t, ALU.mult)

            step(dve.memset(ones[:], 1.0))
            for c in range(POOL_BUF):
                step(dve.memset(inv_count[:, c:c + 1], 1.0 / (c + 1)))
            def stage_x(k):
                dve.wait_ge(x_t, k + 1)
                if k >= 4:
                    dve.wait_ge(spilled[k % 4], 16 * (k // 4))
                    dve.wait_ge(x_hi, k - 3)
                    dve.wait_ge(x_lo, k - 3)
                dve.tensor_copy(scratch[:, k % 4, 0:PROMPT], ps[:, 4 + k % 3, :]).then_inc(x_staged, 1)

            stage_x(0)
            stage_x(1)
            dve.wait_ge(small_t, 2)
            dve.tensor_copy(vec[:, 0:VECTORS], ps[:, 3, 0:VECTORS]).then_inc(small_copied, 1)
            dve.tensor_copy(xs_t[:], ps[:, 3, P:2 * P]).then_inc(small_copied, 1)
            dve.wait_ge(small_copied, 2)
            xs_g = rstd[:, 0:P].rearrange("p (c b) -> p c b", b=SAMPLES)
            dve.tensor_tensor(xs_g, xs_t[:].rearrange("p (b c) -> p c b", b=SAMPLES),
                              vec[:, 0:KC].unsqueeze(2).broadcast_to([P, KC, SAMPLES]), ALU.mult).then_inc(xs_scaled, 1)

            def heads_tail(i, j):
                if j == 2:
                    dve.wait_ge(gates_tanh, 4 * i + 4)
                    dve.scalar_tensor_tensor(out=xc, in0=tanh_x, scalar=1.0, in1=xc, op0=ALU.add,
                                             op1=ALU.mult).then_inc(xi_ready, 1)
                    dve.wait_ge(decay_exp, 2 * i + 2)
                    step(dve.tensor_scalar(q, q, 0.5, 0.5, ALU.mult, ALU.add))
                if j == 3:
                    dve.wait_ge(unit_used, 16 * i + 16)
                    for h in range(2):
                        dve.tensor_tensor(halves(gate[:, h]), bank(1, h), halves(rstd[:]), ALU.mult).then_inc(gate_evac, 1)
                if j == 4:
                    settle()
                    dve.wait_ge(decay_tanh, 2 * i + 2)
                    dve.scalar_tensor_tensor(out=decay, in0=tanh_a, scalar=1.0, in1=q, op0=ALU.add,
                                             op1=ALU.mult).then_inc(tanh_used, 1)
                    dve.wait_ge(tanh_used, i + 1)
                    step(dve.tensor_scalar(decay, decay, -1.0, 2.0, ALU.mult, ALU.add))
                    settle()
                    step(dve.tensor_tensor(q, q, decay, ALU.mult))
                if j == 5:
                    settle()
                    step(dve.tensor_scalar(decay, q, 2.0, -1.0, ALU.mult, ALU.add))
                    dve.wait_ge(root_t, i + 1)
                    step(dve.tensor_tensor(q, tanh_a, q, ALU.mult))
                    settle()
                    step(dve.memset(q[:, :, 0:1], 0.5))
                if j == 6:
                    settle()
                    dve.wait_ge(xi_ready, i + 1)
                    step(dve.tensor_tensor(xc, xc, q, ALU.mult))
                    dve.wait_ge(gate_sq, i + 1)
                    step(dve.tensor_scalar(tanh_x, tanh_x, GELU_CUBIC, 1.0, ALU.mult, ALU.add))
                    settle()
                    dve.tensor_tensor(tanh_x, tanh_x, gate, ALU.mult).then_inc(gate_arg, 1)
                if j == 7:
                    for h in range(2):
                        step(dve.tensor_tensor_scan(tanh_a[:, h, 0:PROMPT], decay[:, h, 0:PROMPT], xc[:, h, 0:PROMPT],
                                                    0.0, ALU.mult, ALU.add))
                    h0 = states[:, 0:64].rearrange("p (b c) -> p c b", b=SAMPLES)[:, bass.ds(2 * i, 2), :]
                    step(dve.tensor_tensor(tanh_a[:, :, PROMPT:TOK], decay[:, :, PROMPT:TOK], h0, ALU.mult))
                    settle()
                    step(dve.tensor_tensor(tanh_a[:, :, PROMPT:TOK], tanh_a[:, :, PROMPT:TOK], xc[:, :, PROMPT:TOK], ALU.add))
                    settle()
                    step(dve.tensor_copy(lru_last[:].rearrange("p j c -> p c j")[:, bass.ds(2 * i, 2), :],
                                         tanh_a[:, :, PROMPT - 1:TOK]))
                if j == 8:
                    dve.wait_ge(gate_th, i + 1)
                    step(dve.scalar_tensor_tensor(out=gate, in0=tanh_x, scalar=1.0, in1=gate, op0=ALU.add, op1=ALU.mult))
                    settle()
                    dve.scalar_tensor_tensor(out=gate, in0=tanh_a, scalar=0.5, in1=gate, op0=ALU.mult,
                                             op1=ALU.mult).then_inc(lru_y, 1)
                if j == 9:
                    dve.wait_ge(y_hi, i + 1)
                    dve.tensor_tensor(y_low[:, bass.ds(2 * i, 2), :], gate, y_high[:, bass.ds(2 * i, 2), :].bitcast(F32),
                                      ALU.subtract).then_inc(y_lo, 1)

            TAIL_STEPS = 14

            def gate_slot(i, j):
                if j == 0:
                    convert_aux(i)
                if j == 3:
                    step(dve.memset(conv_in[:, :, 0:3], 0.0))
                    for h in range(2):
                        old = states[:, ST_CONV:ST_POOL].rearrange("p (b k c) -> p c b k", b=SAMPLES, k=3)
                        new = conv_in[:, h, EXT_S:EXT_S + CONV_W * SAMPLES].rearrange("p (b k) -> p b k", k=CONV_W)
                        step(dve.tensor_copy(new[:, :, 0:3].unsqueeze(1), old[:, bass.ds(2 * i + h, 1)]))
                    dve.wait_ge(unit_used, 16 * i + 8)
                    for h in range(2):
                        step(dve.tensor_tensor(halves(conv_in[:, h, 3:3 + TOK]), bank(0, h), halves(rstd[:]), ALU.mult))
                    settle()
                    ext = conv_in[:, :, EXT_S:EXT_S + CONV_W * SAMPLES].rearrange("p h (b k) -> p h b k", k=CONV_W)
                    dve.tensor_copy(ext[:, :, :, 3], conv_in[:, :, 3 + PROMPT:3 + TOK]).then_inc(ext_ready, 1)
                if j == 4:
                    for k in range(1, 3):
                        for h in range(2):
                            if k == 1:
                                dve.wait_ge(ext_ready, i + 1)
                                dve.wait_ge(tap0_ready, 2 * i + (h + 1))
                            step(dve.scalar_tensor_tensor(out=conv_sum[:, h], in0=conv_in[:, h, k:k + CONV],
                                                          scalar=column("conv_w", 2 * i + h + k * HEADS),
                                                          in1=conv_sum[:, h], op0=ALU.mult, op1=ALU.add))
                        settle()
                if j == 5:
                    for h in range(2):
                        w3 = column("conv_w", 2 * i + h + 3 * HEADS)
                        step(dve.scalar_tensor_tensor(out=xc[:, h, 0:PROMPT], in0=conv_in[:, h, 3:3 + PROMPT], scalar=w3,
                                                      in1=conv_sum[:, h, 0:PROMPT], op0=ALU.mult, op1=ALU.add))
                        ins = dve.scalar_tensor_tensor(
                            out=xc[:, h, PROMPT:TOK], in0=conv_in[:, h, 3 + PROMPT:3 + TOK], scalar=w3,
                            in1=conv_sum[:, h, EXT_S:EXT_S + CONV_W * (SAMPLES - 1) + 1:CONV_W],
                            op0=ALU.mult, op1=ALU.add)
                        if h == 0:
                            step(ins)
                    ins.then_inc(xc_ready, 1)
                if j == 6:
                    step(dve.tensor_copy(conv_last[:].rearrange("p j c -> p c j")[:, bass.ds(2 * i, 2), :],
                                         conv_in[:, :, PROMPT:3 + TOK]))
                    settle()
                    dve.wait_ge(xc_hi, i + 1)
                    dve.tensor_tensor(y_low[:, bass.ds(2 * i, 2), :], xc, y_high[:, bass.ds(2 * i, 2), :].bitcast(F32),
                                      ALU.subtract).then_inc(xc_lo, 1)

            GATE_STEPS = 5 + 4 + 3 + 1

            def softplus(part):
                lam = vec[:, ROWS_OF["lam"]:ROWS_OF["lam"] + HEADS]
                t, e, s, p = (tiny[:, m, :] for m in (1, 0, 2, 3))
                settle()
                if part == 0:
                    dve.wait_ge(lam_tanh, 1)
                    step(dve.tensor_scalar(s, t, 1.0, None, ALU.add))
                    settle()
                    step(dve.reciprocal(p, s))
                    step(dve.tensor_scalar(e, t, -1.0, 1.0, ALU.mult, ALU.add))
                    settle()
                    step(dve.tensor_tensor(e, e, p, ALU.mult))
                if part == 1:
                    for _ in range(4):
                        step(dve.tensor_tensor(e, e, e, ALU.mult))
                        settle()
                    step(dve.tensor_scalar(s, e, 2.0, None, ALU.add))
                    settle()
                    step(dve.reciprocal(p, s))
                if part == 2:
                    step(dve.tensor_tensor(s, e, p, ALU.mult))
                    settle()
                    step(dve.tensor_tensor(t, s, s, ALU.mult))
                    settle()
                    step(dve.tensor_scalar(p, t, 1.0 / 17.0, None, ALU.mult))
                    settle()
                    for odd in (15, 13, 11):
                        step(dve.scalar_tensor_tensor(out=p, in0=p, scalar=1.0 / odd, in1=t, op0=ALU.add, op1=ALU.mult))
                        settle()
                if part == 3:
                    for odd in (9, 7, 5, 3):
                        step(dve.scalar_tensor_tensor(out=p, in0=p, scalar=1.0 / odd, in1=t, op0=ALU.add, op1=ALU.mult))
                        settle()
                    step(dve.scalar_tensor_tensor(out=s, in0=p, scalar=1.0, in1=s, op0=ALU.add, op1=ALU.mult))
                    step(dve.tensor_scalar(e, lam, -1.0, 0.0, ALU.mult, ALU.max))
                    settle()
                    step(dve.scalar_tensor_tensor(out=e, in0=s, scalar=2.0, in1=e, op0=ALU.mult, op1=ALU.add))
                    settle()
                    step(dve.tensor_scalar(lru_c[:, 0, :], e, 2.0, None, ALU.mult))
                    step(dve.tensor_scalar(lru_c[:, 1, :], e, -4.0, None, ALU.mult))

            lam = vec[:, ROWS_OF["lam"]:ROWS_OF["lam"] + HEADS]
            b_a = ROWS_OF["b_a"]
            step(dve.tensor_scalar(half_bias[:], vec[:, b_a:b_a + 2 * HEADS], 0.5, None, ALU.mult))
            dve.scalar_tensor_tensor(out=tiny[:, 0, :], in0=lam, scalar=-1.0, in1=lam, op0=ALU.mult,
                                     op1=ALU.max).then_inc(lam_ready, 1)
            for j in range(PAIR_UNITS):
                convert(0, j, j < RING)
                if j == PAIR_UNITS - 1:
                    dve.wait_ge(sumsq_ready, 17)
                    dve.wait_ge(xs_lo, 1)
                    step(dve.tensor_reduce(sumsq[:, 0:4], sq_parts[:], AX_X, ALU.add))
                    settle()
                    for t in range(4):
                        dve.tensor_scalar(rstd[:, t * P:(t + 1) * P], ident[:], sumsq[:, t:t + 1], None,
                                          ALU.mult).then_inc(diag_ready, 1)
                    dve.tensor_scalar(rstd[:, PROMPT:TOK], sel[:], sumsq[:, 4:5], None, ALU.mult).then_inc(diag_ready, 1)
                for k in (2 * j, 2 * j + 1):
                    dve.wait_ge(x_hi, k + 1)
                    dve.wait_ge(x_staged, k + 1)
                    dve.scalar_tensor_tensor(out=h_low[:, k, 0:PROMPT], in0=scratch[:, k % 4, 0:PROMPT],
                                             scalar=column("g_mix", k),
                                             in1=h_high[:, k, 0:PROMPT].bitcast(F32), op0=ALU.mult,
                                             op1=ALU.subtract).then_inc(x_lo, 1)
                if j == 0:
                    dve.wait_ge(xs_hi, 1)
                    dve.tensor_tensor(h_low[:, :, PROMPT:TOK], xs_g, h_high[:, :, PROMPT:TOK].bitcast(F32),
                                      ALU.subtract).then_inc(xs_lo, 1)
                    dve.wait_ge(ident_ready, 2)
                    step(dve.tensor_reduce(sel[:], ident[:].rearrange("p (b c) -> p b c", b=SAMPLES), AX_X, ALU.add))
                if 1 <= j <= 4:
                    softplus(j - 1)
                for k in (2 * j + 2, 2 * j + 3):
                    if k < KC:
                        stage_x(k)
            for j in range(PAIR_UNITS):
                convert(1, j)
                if j == 2:
                    dve.wait_ge(states_t, 1)
                    dve.tensor_copy(states[:, 0:ST_POOL], ps[:, 4, 0:ST_POOL]).then_inc(states_copied, 1)
                    for s in spilled[0:2]:
                        dve.wait_ge(s, 64)
                    dve.wait_ge(total_ready, 1)
                    step(dve.tensor_scalar(scratch[:, 0, 0:PROMPT], ps[:, 7, :], 1.0 / D, EPS, ALU.mult, ALU.add))
                    dve.tensor_scalar(scratch[:, 0, PROMPT:TOK], ps[:, 4, 504:512], 1.0 / D, EPS, ALU.mult,
                                      ALU.add).then_inc(mean_ready, 1)
                    dve.wait_ge(states_copied, 2)
                    dve.wait_ge(mean_ready, 1)
                    dve.wait_ge(root_ready, 1)
                    settle()
                    step(newton(rstd[:], scratch[:, 0, :], scratch[:, 1, :], scratch[:, 1, :]))
                    settle()
                gate_slot(0, j)
            with dve.Fori(1, 4) as i:
                order.enter(i - 1, TAIL_STEPS + GATE_STEPS)
                for j in range(PAIR_UNITS):
                    convert(2 * i, j)
                    heads_tail(i - 1, j)
                for j in range(PAIR_UNITS):
                    convert(2 * i + 1, j)
                    heads_tail(i - 1, PAIR_UNITS + j)
                    gate_slot(i, j)
                order.leave(3)

            def pool_result(n):
                for t in range(2):
                    dve.wait_ge(y_hi, 4 + 2 * n + t + 1)
                    y = HEADS + 2 * n + t
                    ins = dve.scalar_tensor_tensor(out=halves(y_low[:, y, :]), in0=bank(n % 2, t),
                                                   scalar=column("pool_scale", 2 * pool_group(n) + t),
                                                   in1=halves(y_high[:, y, :]).bitcast(F32), op0=ALU.mult, op1=ALU.subtract)
                    ins.then_inc(y_lo, 1)
                dve.wait_ge(y_lo, 4 + 2 * n + 2)
                dve.memset(sel[:, 0:1], 0.0).then_inc(pair_evac, 1)

            def pool_steps(n, j):
                g = pool_group(n)
                w = WINDOWS[g]
                ext = pool_in[:, :, PEXT_S:PEXT].rearrange("p t (b k) -> p t b k", k=POOL_BUF + 1)
                if j == 3:
                    if n == 0:
                        dve.wait_ge(y_lo, 4)
                    else:
                        dve.wait_ge(pooled_lo, n)
                        dve.wait_ge(pooled_ready, n)
                    settle()
                    step(dve.memset(pool_in[:, :, 0:POOL_BUF], 0.0))
                    for t in range(2):
                        old = states[:, ST_POOL:ST_COLS].rearrange("p (b k c) -> p c b k", b=SAMPLES, k=POOL_BUF)
                        step(dve.tensor_copy(ext[:, t, :, 0:POOL_BUF], old[:, 2 * g + t]))
                    dve.wait_ge(unit_used, 8 * (9 + n))
                    for t in range(2):
                        step(dve.tensor_tensor(halves(pool_in[:, t, POOL_BUF:POOL_BUF + TOK]), bank(n % 2, t), halves(rstd[:]),
                                               ALU.mult))
                    settle()
                    step(dve.tensor_copy(ext[:, :, :, POOL_BUF], pool_in[:, :, POOL_BUF + PROMPT:POOL_BUF + TOK]))
                    settle()
                    step(dve.tensor_copy(pool_last[:].rearrange("p j c -> p c j")[:, 2 * g:2 * g + 2, :],
                                         pool_in[:, :, PROMPT:POOL_BUF + TOK]))
                    src, dst, other, width = pool_in, sum_a, sum_b, 1
                    while width < w:
                        cols = PEXT - 2 * width + 1
                        step(dve.tensor_tensor(dst[:, :, 0:cols], src[:, :, 0:cols], src[:, :, width:width + cols], ALU.add))
                        settle()
                        src, dst, other, width = dst, other, dst, 2 * width
                    pool_steps.sums = src
                if j == 5:
                    sums = pool_steps.sums
                    start = POOL_BUF + 1 - w
                    sum_ext = sums[:, :, PEXT_S:PEXT].rearrange("p t (b k) -> p t b k", k=POOL_BUF + 1)
                    if n >= 1:
                        dve.wait_ge(pooled_hi, n)
                    step(dve.scalar_tensor_tensor(out=pooled[:, :, 0:PROMPT], in0=sums[:, :, start:start + PROMPT],
                                                  scalar=1.0 / w, in1=pool_in[:, :, POOL_BUF:POOL_BUF + PROMPT],
                                                  op0=ALU.mult, op1=ALU.subtract))
                    step(dve.scalar_tensor_tensor(out=pooled[:, :, PROMPT:TOK], in0=sum_ext[:, :, :, start], scalar=1.0 / w,
                                                  in1=pool_in[:, :, POOL_BUF + PROMPT:POOL_BUF + TOK],
                                                  op0=ALU.mult, op1=ALU.subtract))
                    for t in range(2):
                        step(dve.tensor_tensor(head_fix[:, t, 0:w - 1], sums[:, t, start:start + w - 1],
                                               inv_count[:, 0:w - 1], ALU.mult))
                    settle()
                    dve.tensor_tensor(pooled[:, :, 0:w - 1], head_fix[:, :, 0:w - 1],
                                      pool_in[:, :, POOL_BUF:POOL_BUF + w - 1], ALU.subtract).then_inc(pooled_ready, 1)
                if j == 6:
                    y = HEADS + 2 * n
                    dve.wait_ge(pooled_hi, n + 1)
                    dve.tensor_tensor(y_low[:, y:y + 2, :], pooled, y_high[:, y:y + 2, :].bitcast(F32),
                                      ALU.subtract).then_inc(pooled_lo, 1)

            def pool_slot(n, j):
                if j == 2 and n >= 2:
                    pool_result(n - 2)
                if j == 2 and n >= 1:
                    convert_aux(3 + n)
                if n >= 1:
                    pool_steps(n - 1, j)

            for n in range(4):
                for j in range(PAIR_UNITS):
                    convert(8 + n, j)
                    if n < 2:
                        heads_tail(3, PAIR_UNITS * n + j)
                    pool_slot(n, j)

            def add_pair(buf, p):
                r = resid[:, bass.ds(2 * p, 2), :].rearrange("p k (a t) -> p k a t", a=2)
                dve.tensor_tensor(r, ps[:, 4 * buf:4 * buf + 4, 0:HALF].rearrange("p (k a) t -> p k a t", a=2), r,
                                  ALU.add).then_inc(pair_evac, 1)

            def out_steps(o, buf):
                dve.wait_ge(unit_used, 8 * o + 104)
                add_pair(buf, o)
                for t in range(2):
                    c = 2 * o + t
                    dve.wait_ge(h2_hi, c + 1)
                    dve.scalar_tensor_tensor(out=h_low[:, bass.ds(c, 1), :].rearrange("p k t -> p (k t)"),
                                             in0=resid[:, bass.ds(c, 1), :].rearrange("p k t -> p (k t)"),
                                             scalar=column("g_mlp", c),
                                             in1=h_high[:, bass.ds(c, 1), :].rearrange("p k t -> p (k t)").bitcast(F32),
                                             op0=ALU.mult, op1=ALU.subtract).then_inc(h2_lo, 1)
                dve.wait_ge(out_sq, o + 1)
                if isinstance(o, int) and o == 0:
                    dve.memset(sel[:, 0:1], 0.0).then_inc(sq_summed, 1)
                else:
                    dve.wait_ge(sq_summed, o)
                    dve.tensor_tensor(scratch[:, 2:4, :], scratch[:, 2:4, :], scratch[:, 0:2, :], ALU.add).then_inc(sq_summed, 1)

            for n in range(2):
                for j in range(PAIR_UNITS):
                    convert(IN_PAIRS + n, j)
                    if n == 0:
                        pool_slot(4, j)
                        if j == 6:
                            dve.wait_ge(pooled_lo, 4)
                            settle()
                            dve.memset(sel[:, 0:1], 0.0).then_inc(last_ready, 1)
                        if j == 7:
                            pool_result(3)
                    elif j == 2:
                        dve.wait_ge(last_t, 4)
                        for m, rows in enumerate((72, 88, 120, 64)):
                            dve.tensor_copy(aux_raw[0:rows, m * P:(m + 1) * P], ps[0:rows, 4 + m, 0:P]).then_inc(last_copied, 1)
                        step(dve.tensor_copy(resid[:, :, PROMPT:TOK], xs_t[:].rearrange("p (b c) -> p c b", b=SAMPLES)))
                        dve.wait_ge(x_back, 64)
                        settle()
                    elif j == 4:
                        out_steps(0, 0)
            with dve.Fori(1, OUT_PAIRS // 2) as b:
                for half in range(2):
                    for j in range(PAIR_UNITS):
                        convert(2 * b + (IN_PAIRS + half), j)
                        if j == 4:
                            out_steps(2 * b + (half - 1), 1 - half)

            def up_steps(m, buf):
                for t in range(2):
                    dve.scalar_tensor_tensor(out=halves(scratch[:, t, :]), in0=bank(buf, t), scalar=0.0, in1=halves(rstd[:]),
                                             op0=ALU.max, op1=ALU.mult).then_inc(f_relu, 1)

            def up_low(m, p):
                dve.wait_ge(f_relu, 2 * m + 2)
                dve.wait_ge(f_hi, m + 1)
                dve.memset(sel[:, 0:1], 0.0).then_inc(pair_evac, 1)
                dve.tensor_tensor(y_low[:, bass.ds(2 * p, 2), :], scratch[:, 0:2, :],
                                  y_high[:, bass.ds(2 * p, 2), :].bitcast(F32), ALU.subtract).then_inc(f_lo, 1)

            def up(g, p, buf):
                dve.wait_ge(unit_used, 128 * g + 8 * p + 168)
                up_steps(8 * g + p, buf)
                up_low(8 * g + p, p)

            def down(g, p, buf):
                dve.wait_ge(unit_used, 128 * g + 8 * p + 232)
                add_pair(buf, p)

            def final(p):
                if p == 0:
                    dve.wait_ge(out_sq, OUT_PAIRS + 1)
                    dve.memset(sel[:, 0:1], 0.0).then_inc(final_sq, 1)
                else:
                    dve.wait_ge(out_sq, OUT_PAIRS + 1 + p)
                    dve.wait_ge(final_sq, p)
                    dve.tensor_tensor(scratch[:, 2:4, :], scratch[:, 2:4, :], scratch[:, 0:2, :], ALU.add).then_inc(final_sq, 1)

            def quarter(g, before, last, between=None):
                for j in range(PAIR_UNITS):
                    convert(16 * g + 20, j)
                    if j == 3:
                        before()
                for j in range(PAIR_UNITS):
                    convert(16 * g + 21, j)
                    if j == 0 and between is not None:
                        between()
                    if j == 4:
                        up(g, 0, 0)
                with dve.Fori(1, MLP_PAIRS // 2) as b:
                    for half in range(2):
                        for j in range(PAIR_UNITS):
                            convert(16 * g + 2 * b + (20 + half), j)
                            if j == 4:
                                up(g, 2 * b + (half - 1), 1 - half)
                for j in range(PAIR_UNITS):
                    convert(16 * g + 28, j)
                    if j == 3:
                        up(g, 7, 1)
                for j in range(PAIR_UNITS):
                    convert(16 * g + 29, j)
                    if j == 4:
                        down(g, 0, 0)
                        if last:
                            final(0)
                if not last:
                    with dve.Fori(1, MLP_PAIRS // 2) as b:
                        for half in range(2):
                            for j in range(PAIR_UNITS):
                                convert(16 * g + 2 * b + (28 + half), j)
                                if j == 4:
                                    down(g, 2 * b + (half - 1), 1 - half)
                else:
                    for p in range(2, MLP_PAIRS):
                        for j in range(PAIR_UNITS):
                            convert(16 * g + p + 28, j)
                            if j == 4:
                                down(g, p - 1, (p - 1) % 2)
                                final(p - 1)
                    dve.wait_ge(final_sq, OUT_PAIRS - 1)
                    dve.wait_ge(states_stored, 16 * (6 + 2 * SAMPLES))
                    a, b = (scratch[:, 2 + t, PROMPT:TOK].unsqueeze(2).broadcast_to([P, SAMPLES, KC]) for t in range(2))
                    dve.tensor_tensor(sample_squares[:, 0, :].rearrange("p (b c) -> p b c", b=SAMPLES), a, b,
                                      ALU.add).then_inc(samples_sq, 1)

            def mlp_norm():
                dve.wait_ge(total_ready, 2)
                dve.tensor_scalar(halves(scratch[:, 0, :]), ps[:, 4:6, 0:HALF], 1.0 / D, EPS, ALU.mult,
                                  ALU.add).then_inc(mean_ready, 1)
                dve.wait_ge(root_ready, 2)
                dve.wait_ge(mean_ready, 2)
                step(newton(rstd[:], scratch[:, 0, :], scratch[:, 1, :], scratch[:, 1, :]))
                settle()

            quarter(0, lambda: out_steps(OUT_PAIRS - 1, 1), False, mlp_norm)
            with dve.Fori(1, GROUPS - 1) as g:
                quarter(g, lambda: down(g - 1, 7, 1), False)
            quarter(GROUPS - 1, lambda: down(GROUPS - 2, 7, 1), True)
            dve.wait_ge(unit_used, 672)
            for t, done in enumerate((last_added, pair_evac)):
                dve.tensor_tensor(halves(resid[:, KC - 2 + t, :]), bank(1, t), halves(resid[:, KC - 2 + t, :]),
                                  ALU.add).then_inc(done, 1)
            dve.wait_ge(last_added, 1)
            dve.wait_ge(pair_evac, 76)
            tail = resid[:, KC - 2:KC, PROMPT:TOK].unsqueeze(3).broadcast_to([P, 2, SAMPLES, KC])
            dve.tensor_tensor(sample_squares[:, 1:3, :].rearrange("p a (b c) -> p a b c", b=SAMPLES), tail, tail,
                              ALU.mult).then_inc(samples_sq, 1)
            dve.wait_ge(samples_sq, 2)
            step(dve.tensor_tensor(sample_squares[:, 1, :], sample_squares[:, 1, :], sample_squares[:, 2, :], ALU.add))
            settle()
            dve.tensor_tensor(sample_squares[:, 0, :], sample_squares[:, 0, :], sample_squares[:, 1, :],
                              ALU.add).then_inc(samples_sq, 1)
            dve.wait_ge(final_total, 1)
            step(dve.tensor_copy(r_final[:, 1, :], ps[:, 0, 4:9]))
            settle()
            step(dve.tensor_tensor(r_final[:, 1, 0:4], r_final[:, 1, 0:4], ps[:, 0, 0:4], ALU.add))
            settle()
            dve.tensor_scalar(r_final[:, 0, :], r_final[:, 1, :], 1.0 / D, EPS, ALU.mult, ALU.add).then_inc(final_rstd, 1)
            dve.wait_ge(final_rstd, 1)
            dve.wait_ge(root_ready, 3)
            newton(r_final[:, 3, :], r_final[:, 0, :], r_final[:, 2, :], r_final[:, 1, :]).then_inc(final_rstd, 1)
            dve.wait_ge(final_rstd, 2)
            for m in range(1, 16, 2):
                dve.wait_ge(y_t, 4 * (m // 4) + 4)
                dve.tensor_scalar(y_rows[:, m, :], ps[:, 1 + m % 7, :], r_final[:, 3, m % 4:m % 4 + 1], None,
                                  ALU.mult).then_inc(y_odd, 1)


_INS = ["x_prompt", "x_sample", "state_lru_h", "state_conv", "state_pool", "norm_mix_g", "w_in", "conv_w", "conv_b",
        "w_rg_a", "b_rg_a", "w_rg_x", "b_rg_x", "lru_lambda", "w_pool", "pool_scale", "w_out", "norm_mlp_g", "w_up",
        "w_down", "norm_final_g"]
_OUTS = [(1, 512, 2048), (8, 1, 2048), (1, 1, 1024), (1, 1, 3, 1024), (1, 1, 15, 1024), (1, 8, 1024), (1, 8, 3, 1024),
         (1, 8, 15, 1024)]


def kernel(**inputs):
    import numpy as _np
    import concourse.bacc as _bacc
    from concourse import mybir as _mybir
    from concourse.bass_utils import run_bass_kernel_spmd as _run

    nc = _bacc.Bacc("TRN2", target_bir_lowering=False, num_devices=1)
    arrays, args = {}, []
    for name in _INS:
        a = _np.ascontiguousarray(inputs[name])
        arrays[f"in_{name}_dram"] = a
        args.append(nc.dram_tensor(f"in_{name}_dram", a.shape, _mybir.dt.from_np(a.dtype), kind="ExternalInput").ap())
    for i, shape in enumerate(_OUTS):
        args.append(nc.dram_tensor(f"out_{i}_dram", shape, _mybir.dt.float32, kind="ExternalOutput").ap())
    build(nc, *args)
    r = _run(nc, [arrays], core_ids=[0])
    return tuple(r.results[0][f"out_{i}_dram"] for i in range(len(_OUTS)))
```
